# Optimizing a Trainium2 kernel written in Bass

```python
import math
import functools
import jax, jax.numpy as jnp
from jax import lax
import numpy as np

D_MODEL = 1024
BATCH = 1
SEQ = 512
DEPTH = 1
DEC_BATCH = 8
DEC_SEQ = 1
PAST_LEN = 2048
PAGE_SIZE = 128

MLA_HEADS = 16
Q_LORA = 384
KV_LORA = 256
NOPE_DIM = 64
ROPE_DIM = 32
V_DIM = 64
ROPE_THETA = 10000.0
Q_BLOCK = 128
SM_SCALE = 1.0 / math.sqrt(NOPE_DIM + ROPE_DIM)
SSM_EXPAND = 2
D_INNER = SSM_EXPAND * D_MODEL
SSM_HEAD_DIM = 64
SSM_HEADS = D_INNER // SSM_HEAD_DIM
SSM_GROUPS = 8
HEADS_PER_GROUP = SSM_HEADS // SSM_GROUPS
D_STATE = 128
CONV_W = 4
CONV_DIM = D_INNER + 2 * SSM_GROUPS * D_STATE
SSD_CHUNK = 128
D_FF = 4 * D_MODEL
EPS = 1e-6
IN_SPLITS = (Q_LORA, KV_LORA, ROPE_DIM, D_INNER, CONV_DIM, SSM_HEADS, D_MODEL, D_MODEL)
D_IN_PROJ = sum(IN_SPLITS)

kernel_name = "hybrid_mla_ssd_gated_decode_step"

def _rms_scale(x):
    xf = x.astype(jnp.float32)
    return xf * lax.rsqrt(jnp.mean(xf * xf, axis=-1, keepdims=True) + EPS)

def _rmsnorm(x, g):
    return (_rms_scale(x) * g.astype(jnp.float32)).astype(x.dtype)

def _split_in(p):
    bounds = [int(v) for v in np.cumsum(IN_SPLITS)[:-1]]
    return jnp.split(p, bounds, axis=-1)

def _rope(x, pos):
    half = ROPE_DIM // 2
    inv_freq = ROPE_THETA ** (-jnp.arange(half, dtype=jnp.float32) / half)
    ang = pos.astype(jnp.float32)[:, None] * inv_freq[None, :]
    cos = jnp.cos(ang)[None, :, None, :]
    sin = jnp.sin(ang)[None, :, None, :]
    xf = x.astype(jnp.float32)
    x1, x2 = xf[..., :half], xf[..., half:]
    return jnp.concatenate([x1 * cos - x2 * sin, x1 * sin + x2 * cos], axis=-1).astype(x.dtype)

def _mla_project(h_q, h_kv, h_pe, pos, g_q, w_uq, g_kv):
    cq = _rmsnorm(h_q, g_q)
    q = jnp.einsum("bsr,rhd->bshd", cq, w_uq)
    q_nope = q[..., :NOPE_DIM]
    q_pe = _rope(q[..., NOPE_DIM:], pos)
    c_kv = _rmsnorm(h_kv, g_kv)
    k_pe = _rope(h_pe[:, :, None, :], pos)[:, :, 0, :]
    return q_nope, q_pe, c_kv, k_pe

def _mla_attend_prompt(q_nope, q_pe, c_kv, k_pe, w_uk, w_uv):
    b, s = q_nope.shape[:2]
    n_blk = s // Q_BLOCK
    k_nope = jnp.einsum("bkr,rhd->bkhd", c_kv, w_uk)
    v = jnp.einsum("bkr,rhd->bkhd", c_kv, w_uv)
    key_pos = jnp.arange(s)
    qn = jnp.moveaxis(q_nope.reshape(b, n_blk, Q_BLOCK, MLA_HEADS, NOPE_DIM), 1, 0)
    qp = jnp.moveaxis(q_pe.reshape(b, n_blk, Q_BLOCK, MLA_HEADS, ROPE_DIM), 1, 0)

    def one_block(args):
        qn_b, qp_b, blk = args
        sc = jnp.einsum("bqhd,bkhd->bhqk", qn_b, k_nope) + jnp.einsum("bqhd,bkd->bhqk", qp_b, k_pe)
        q_pos = blk * Q_BLOCK + jnp.arange(Q_BLOCK)
        sc = jnp.where(key_pos[None, :] <= q_pos[:, None], sc.astype(jnp.float32) * SM_SCALE, -jnp.inf)
        p = jax.nn.softmax(sc, axis=-1).astype(v.dtype)
        return jnp.einsum("bhqk,bkhd->bqhd", p, v)

    o = lax.map(one_block, (qn, qp, jnp.arange(n_blk)))
    return jnp.moveaxis(o, 0, 1).reshape(b, s, MLA_HEADS * V_DIM)

def _mla_attend_sample(q_nope, q_pe, c_kv, k_pe, cache_kv, cache_pe, page_table, w_uk, w_uv):
    b, s = q_nope.shape[:2]
    past_kv = cache_kv[page_table].reshape(b, -1, KV_LORA)
    past_pe = cache_pe[page_table].reshape(b, -1, ROPE_DIM)
    past_len = past_kv.shape[1]
    q_lat = jnp.einsum("bshd,rhd->bshr", q_nope, w_uk)
    sc_past = jnp.einsum("bshr,btr->bhst", q_lat, past_kv) + jnp.einsum("bshd,btd->bhst", q_pe, past_pe)
    sc_new = jnp.einsum("bshr,btr->bhst", q_lat, c_kv) + jnp.einsum("bshd,btd->bhst", q_pe, k_pe)
    causal = jnp.arange(s)[None, :] <= jnp.arange(s)[:, None]
    sc_new = jnp.where(causal, sc_new.astype(jnp.float32) * SM_SCALE, -jnp.inf)
    sc = jnp.concatenate([sc_past.astype(jnp.float32) * SM_SCALE, sc_new], axis=-1)
    p = jax.nn.softmax(sc, axis=-1).astype(c_kv.dtype)
    o_lat = (jnp.einsum("bhst,btr->bshr", p[..., :past_len], past_kv)
             + jnp.einsum("bhst,btr->bshr", p[..., past_len:], c_kv))
    return jnp.einsum("bshr,rhd->bshd", o_lat, w_uv).reshape(b, s, MLA_HEADS * V_DIM)

def _causal_conv(xbc, conv_prev, w_conv, b_conv):
    s = xbc.shape[1]
    full = jnp.concatenate([conv_prev.astype(xbc.dtype), xbc], axis=1)
    acc = b_conv
    for k in range(CONV_W):
        acc = acc + full[:, k:k + s] * w_conv[k]
    return jax.nn.silu(acc), full[:, s:]

def _ssd(x, dt, a, bm, cm, init_state):
    b, s = x.shape[:2]
    t = SSD_CHUNK if s % SSD_CHUNK == 0 else s
    nc = s // t
    G, HG, P, N = SSM_GROUPS, HEADS_PER_GROUP, SSM_HEAD_DIM, D_STATE
    la = (dt * a).reshape(b, nc, t, SSM_HEADS)
    xdt = (x.astype(jnp.float32) * dt[..., None]).reshape(b, nc, t, G, HG, P)
    bc = bm.astype(jnp.float32).reshape(b, nc, t, G, N)
    cc = cm.astype(jnp.float32).reshape(b, nc, t, G, N)
    cs = jnp.cumsum(la, axis=2)
    seg = cs[:, :, :, None, :] - cs[:, :, None, :, :]
    tri = jnp.arange(t)[:, None] >= jnp.arange(t)[None, :]
    decay = jnp.exp(jnp.where(tri[:, :, None], seg, -jnp.inf)).reshape(b, nc, t, t, G, HG)
    cb = jnp.einsum("bclgn,bcsgn->bclsg", cc, bc)
    y_diag = jnp.einsum("bclsgh,bcsghp->bclghp", cb[..., None] * decay, xdt)
    to_end = jnp.exp(cs[:, :, -1:, :] - cs).reshape(b, nc, t, G, HG)
    local = jnp.einsum("bcsgn,bcsgh,bcsghp->bcghpn", bc, to_end, xdt)
    chunk_decay = jnp.exp(cs[:, :, -1, :]).reshape(b, nc, G, HG)

    def step(state, inp):
        dec, loc = inp
        return state * dec[..., None, None] + loc, state

    init = init_state.astype(jnp.float32).reshape(b, G, HG, P, N)
    final, prev = lax.scan(step, init, (jnp.moveaxis(chunk_decay, 1, 0), jnp.moveaxis(local, 1, 0)))
    prev = jnp.moveaxis(prev, 0, 1)
    y_off = jnp.einsum("bclgn,bcghpn,bclgh->bclghp", cc, prev, jnp.exp(cs).reshape(b, nc, t, G, HG))
    y = (y_diag + y_off).reshape(b, s, SSM_HEADS, P)
    return y, final.reshape(b, SSM_HEADS, P, N)

def _ssm_branch(z, xbc_raw, dt_raw, conv_prev, ssm_prev, w_conv, b_conv, dt_bias, a_log, d_skip, g_ssm):
    b, s = z.shape[:2]
    xbc, conv_new = _causal_conv(xbc_raw, conv_prev, w_conv, b_conv)
    xs, bm, cm = jnp.split(xbc, [D_INNER, D_INNER + SSM_GROUPS * D_STATE], axis=-1)
    xs = xs.reshape(b, s, SSM_HEADS, SSM_HEAD_DIM)
    bm = bm.reshape(b, s, SSM_GROUPS, D_STATE)
    cm = cm.reshape(b, s, SSM_GROUPS, D_STATE)
    dt = jax.nn.softplus(dt_raw.astype(jnp.float32) + dt_bias.astype(jnp.float32))
    a = -jnp.exp(a_log.astype(jnp.float32))
    y, ssm_new = _ssd(xs, dt, a, bm, cm, ssm_prev)
    y = y + d_skip.astype(jnp.float32)[:, None] * xs.astype(jnp.float32)
    y = y.reshape(b, s, D_INNER) * jax.nn.silu(z.astype(jnp.float32))
    y = _rms_scale(y.reshape(b, s, SSM_GROUPS, D_INNER // SSM_GROUPS)).reshape(b, s, D_INNER)
    return (y * g_ssm.astype(jnp.float32)).astype(z.dtype), conv_new, ssm_new

def _trunk_layer(x, pos, conv_prev, ssm_prev, attend, p):
    h = _rmsnorm(x, p["g_pre_mix"])
    h_q, h_kv, h_pe, z, xbc_raw, dt_raw, gate_a, gate_b = _split_in(h @ p["w_in"])
    q_nope, q_pe, c_kv, k_pe = _mla_project(h_q, h_kv, h_pe, pos, p["g_q"], p["w_uq"], p["g_kv"])
    o_attn = attend(q_nope, q_pe, c_kv, k_pe)
    o_ssm, conv_new, ssm_new = _ssm_branch(z, xbc_raw, dt_raw, conv_prev, ssm_prev, p["w_conv"], p["b_conv"],
                                           p["dt_bias"], p["a_log"], p["d_skip"], p["g_ssm"])
    merged = jax.nn.sigmoid(gate_a) * (o_attn @ p["w_br_attn"]) + jax.nn.sigmoid(gate_b) * (o_ssm @ p["w_br_ssm"])
    x = x + _rmsnorm(merged @ p["w_out"], p["g_post_mix"])
    h2 = _rmsnorm(x, p["g_pre_mlp"])
    f = jnp.square(jax.nn.relu(h2 @ p["w_up"])) @ p["w_down"]
    x = x + _rmsnorm(f, p["g_post_mlp"])
    return x, c_kv, k_pe, conv_new, ssm_new

def setup_inputs(seed: int = 0) -> dict:
    key = jax.random.key(seed)
    ks = jax.random.split(key, 32)
    f32 = jnp.float32
    n_pages = PAST_LEN // PAGE_SIZE
    n_used = DEC_BATCH * n_pages
    n_phys = n_used + n_used // 4

    def nrm(k, shape, scale):
        return jax.random.normal(k, shape, f32) * scale

    def gain(k, shape):
        return 1.0 + 0.05 * jax.random.normal(k, shape, f32)

    dt0 = jnp.exp(jax.random.uniform(ks[20], (DEPTH, SSM_HEADS), f32, math.log(1e-3), math.log(1e-1)))
    return {
        "x_prompt": nrm(ks[0], (BATCH, SEQ, D_MODEL), 1.0),
        "x_sample": nrm(ks[1], (DEC_BATCH, DEC_SEQ, D_MODEL), 1.0),
        "cache_kv_latent": nrm(ks[2], (DEPTH, n_phys, PAGE_SIZE, KV_LORA), 1.0),
        "cache_k_rope": nrm(ks[3], (DEPTH, n_phys, PAGE_SIZE, ROPE_DIM), 1.0),
        "state_ssm": nrm(ks[4], (DEPTH, DEC_BATCH, SSM_HEADS, SSM_HEAD_DIM, D_STATE), 0.1),
        "state_conv": nrm(ks[5], (DEPTH, DEC_BATCH, CONV_W - 1, CONV_DIM), 1.0),
        "page_table": jax.random.permutation(ks[6], n_phys)[:n_used].reshape(DEC_BATCH, n_pages).astype(jnp.int32),
        "w_in": nrm(ks[7], (DEPTH, D_MODEL, D_IN_PROJ), D_MODEL ** -0.5),
        "g_pre_mix": gain(ks[8], (DEPTH, D_MODEL)),
        "g_q": gain(ks[9], (DEPTH, Q_LORA)),
        "w_uq": nrm(ks[10], (DEPTH, Q_LORA, MLA_HEADS, NOPE_DIM + ROPE_DIM), Q_LORA ** -0.5),
        "g_kv": gain(ks[11], (DEPTH, KV_LORA)),
        "w_uk": nrm(ks[12], (DEPTH, KV_LORA, MLA_HEADS, NOPE_DIM), KV_LORA ** -0.5),
        "w_uv": nrm(ks[13], (DEPTH, KV_LORA, MLA_HEADS, V_DIM), KV_LORA ** -0.5),
        "w_conv": nrm(ks[14], (DEPTH, CONV_W, CONV_DIM), CONV_W ** -0.5),
        "b_conv": nrm(ks[15], (DEPTH, CONV_DIM), 0.02),
        "dt_bias": dt0 + jnp.log(-jnp.expm1(-dt0)),
        "a_log": jnp.log(jax.random.uniform(ks[16], (DEPTH, SSM_HEADS), f32, 1.0, 16.0)),
        "d_skip": gain(ks[17], (DEPTH, SSM_HEADS)),
        "g_ssm": gain(ks[18], (DEPTH, D_INNER)),
        "w_br_attn": nrm(ks[19], (DEPTH, MLA_HEADS * V_DIM, D_MODEL), (MLA_HEADS * V_DIM) ** -0.5),
        "w_br_ssm": nrm(ks[21], (DEPTH, D_INNER, D_MODEL), D_INNER ** -0.5),
        "w_out": nrm(ks[22], (DEPTH, D_MODEL, D_MODEL), D_MODEL ** -0.5),
        "g_post_mix": gain(ks[23], (DEPTH, D_MODEL)),
        "g_pre_mlp": gain(ks[24], (DEPTH, D_MODEL)),
        "w_up": nrm(ks[25], (DEPTH, D_MODEL, D_FF), D_MODEL ** -0.5),
        "w_down": nrm(ks[26], (DEPTH, D_FF, D_MODEL), D_FF ** -0.5),
        "g_post_mlp": gain(ks[27], (DEPTH, D_MODEL)),
    }

def reference(x_prompt, x_sample, cache_kv_latent, cache_k_rope, state_ssm, state_conv, page_table,
              w_in, g_pre_mix, g_q, w_uq, g_kv, w_uk, w_uv, w_conv, b_conv, dt_bias, a_log, d_skip, g_ssm,
              w_br_attn, w_br_ssm, w_out, g_post_mix, g_pre_mlp, w_up, w_down, g_post_mlp):
    b_p, s_p = x_prompt.shape[:2]
    b_s, s_s = x_sample.shape[:2]
    past_len = page_table.shape[1] * PAGE_SIZE
    pos_prompt = jnp.arange(s_p, dtype=jnp.int32)
    pos_sample = past_len + jnp.arange(s_s, dtype=jnp.int32)
    conv_zero = jnp.zeros((b_p, CONV_W - 1, CONV_DIM), x_prompt.dtype)
    ssm_zero = jnp.zeros((b_p, SSM_HEADS, SSM_HEAD_DIM, D_STATE), jnp.float32)

    kvp, kpp, ssp, cvp, kvs, kps, sss, cvs = [], [], [], [], [], [], [], []
    xp, xs = x_prompt, x_sample
    for l in range(DEPTH):
        p = dict(w_in=w_in[l], g_pre_mix=g_pre_mix[l], g_q=g_q[l], w_uq=w_uq[l], g_kv=g_kv[l],
                 w_conv=w_conv[l], b_conv=b_conv[l], dt_bias=dt_bias[l], a_log=a_log[l], d_skip=d_skip[l],
                 g_ssm=g_ssm[l], w_br_attn=w_br_attn[l], w_br_ssm=w_br_ssm[l], w_out=w_out[l],
                 g_post_mix=g_post_mix[l], g_pre_mlp=g_pre_mlp[l], w_up=w_up[l], w_down=w_down[l],
                 g_post_mlp=g_post_mlp[l])
        attend_p = functools.partial(_mla_attend_prompt, w_uk=w_uk[l], w_uv=w_uv[l])
        attend_s = functools.partial(_mla_attend_sample, cache_kv=cache_kv_latent[l], cache_pe=cache_k_rope[l],
                                     page_table=page_table, w_uk=w_uk[l], w_uv=w_uv[l])
        xp, ckv_p, kpe_p, conv_p, ssm_p = _trunk_layer(xp, pos_prompt, conv_zero, ssm_zero, attend_p, p)
        xs, ckv_s, kpe_s, conv_s, ssm_s = _trunk_layer(xs, pos_sample, state_conv[l], state_ssm[l], attend_s, p)
        kvp.append(ckv_p); kpp.append(kpe_p); ssp.append(ssm_p); cvp.append(conv_p)
        kvs.append(ckv_s); kps.append(kpe_s); sss.append(ssm_s); cvs.append(conv_s)

    return (xp, xs,
            jnp.stack(kvp), jnp.stack(kpp), jnp.stack(ssp), jnp.stack(cvp),
            jnp.stack(kvs), jnp.stack(kps), jnp.stack(sss), jnp.stack(cvs))


_drawn_inputs = setup_inputs


def setup_inputs(seed=0):
    import zlib

    import numpy as np

    out = dict(_drawn_inputs(seed))
    spreads = {}
    factors = {'cache_k_rope': 3.88, 'g_q': 8.0, 'd_skip': 3.295}
    for name, (base, spread) in spreads.items():
        noise = np.random.default_rng([zlib.crc32(name.encode()), seed]).standard_normal(out[name].shape)
        drawn = base * np.exp(spread * noise) if base else spread * noise
        out[name] = __import__('jax').numpy.asarray(drawn.astype(out[name].dtype))
    for name, factor in factors.items():
        out[name] = (out[name] * factor).astype(out[name].dtype)
    return out
```

```python
import numpy as np
import concourse.bass as bass
from concourse import mybir
from contextlib import ExitStack

F32 = mybir.dt.float32
F32R = mybir.dt.float32r
I32 = mybir.dt.int32
ALU = mybir.AluOpType
ACT = mybir.ActivationFunctionType
AX = mybir.AxisListType

P = 128
D_MODEL, SEQ, NB = 1024, 512, 8
T = SEQ + NB
HALF = T // 2
PAST, PAGE = 2048, 128
HEADS, Q_LORA, KV_LORA, NOPE, ROPE, V_DIM = 16, 384, 256, 64, 32, 64
D_INNER, SSM_HEADS, GROUPS, STATE, CONV_W = 2048, 32, 8, 128, 4
HPG = SSM_HEADS // GROUPS
CONV_DIM = D_INNER + 2 * GROUPS * STATE
D_FF = 4096
EPS = 1e-6
SM_SCALE = 1.0 / float(np.sqrt(NOPE + ROPE))
NEG = -1e30
CHUNK = 128
NCH = SEQ // CHUNK
KT = D_MODEL // P
TOKT = 65
N_PHYS = 160
PAGES = PAST // PAGE
RAWW = 3 + SEQ + 4 * NB
CONVW = RAWW - 3
SAMP0 = SEQ + 3

IN_LIN = ["x0", "x1", "b", "c", "z0", "z1"]
HEAD_LIN = ["uq0", "uq1", "uk", "uv", "ql", "bB", "bC"]
TAIL_LIN = ["bc"] + [f"s{m}" for m in range(8)]
FIRST_LIN = IN_LIN
STEADY_LIN = HEAD_LIN + ["sA0", "x0", "sA1", "x1", "sA2", "b", "sA3", "c", "z0", "z1"] + TAIL_LIN
LAST_LIN = HEAD_LIN + ["sA0", "sA1", "sA2", "sA3"] + TAIL_LIN
FIRST_CH = IN_LIN
STEADY_CH = ["UQ", "UKV"] + IN_LIN + ["SA", "SB"]
LAST_CH = ["UQ", "UKV", "SA", "SB"]
PRE_LIN = ["bcx", "misc", "q0", "q1", "q2", "kv0", "kv1", "bcq", "bckv"]
PRE_CH = ["misc", "q0", "q1", "q2", "kv0", "kv1"]

ROW_LIN = ["SN", "ga", "gb", "PT", "PN", "OL"]
LIN_C = len(PRE_LIN)
LIN_D = LIN_C + len(FIRST_LIN) + 7 * len(STEADY_LIN) + len(LAST_LIN)
LIN_OV = LIN_D + NB * len(ROW_LIN)
LIN_E = LIN_OV + 1
LIN_F = LIN_E + KT
LIN_N = LIN_F + KT
LIN_G = LIN_N + 2
LIN_H = LIN_G + 8 * 12
CH_C = len(PRE_CH)
CH_D = CH_C + len(FIRST_CH) + 7 * len(STEADY_CH) + len(LAST_CH)
CH_OV = CH_D + 2 * NB
CH_E = CH_OV + 2
CH_F = CH_E + KT
CH_G = CH_F + KT
N_CHUNKS = CH_G + 8 * 8


GROUP_LINKS = 67
ROW_LINKS = 4


class Place:

    def __init__(self, index, slot, turn):
        self.index, self.slot, self.turn = index, slot, turn

    def next(self):
        return Place(self.index + 1, 1 - self.slot, self.turn + self.slot)


def fixed(n):
    return Place(n, n % 2, n // 2)


def looped(base, per, i, k):
    return Place(i * per + (base + k), (base + k) % 2, i * (per // 2) + (base + k) // 2)


def c_place(base, first, steady, last, i, name):
    if isinstance(i, int) and i == 0:
        return fixed(base + first.index(name))
    start = base + len(first)
    if isinstance(i, int) and i == GROUPS:
        return fixed(start + 7 * len(steady) + last.index(name))
    return looped(start, len(steady), i - 1, steady.index(name))


def c_lin(i, name):
    return c_place(LIN_C, FIRST_LIN, STEADY_LIN, LAST_LIN, i, name)


def c_chunk(i, name):
    return c_place(CH_C, FIRST_CH, STEADY_CH, LAST_CH, i, name)


class Chain:

    def __init__(self, eng, sem):
        self.eng, self.sem, self.base, self.local, self.i, self.per = eng, sem, 0, 0, 0, 0

    def link(self, ins):
        self.local += 1
        ins.then_inc(self.sem, 1)
        self.eng.wait_ge(self.sem, self.i * self.per + (self.base + self.local))

    def enter(self, i, per):
        self.base += self.local
        self.local, self.i, self.per = 0, i, per

    def leave(self, trips):
        assert self.local == self.per, f"links per iteration: {self.local}, stated {self.per}"
        self.base += trips * self.per
        self.local, self.i, self.per = 0, 0, 0


SMALL = {}
ARENA = 16708
SEMAPHORES = """w_loaded0 w_loaded1 w_split w_used w_hi_done dve_chain act_chain lin_done lin_free
    x_in consts_in ones_set pe_gate sp_gate exp_alog sq_x stat_done rstd_diag norm_val norm_hi act_ready
    dt_raw kpe_ready lat_sq sp_ln cs_ready rows_tr rows_ready kv_val kv_out kpe_out arena_free
    hist_in conv_out raw_act conv_acc conv_tanh xc_ready qbd_hi_s q_ready k_act v_act
    sdm_ready sdec_mm st_in0 st_in1 st_new st_out0 st_out1 scores max_bias exp_done prob_ready
    pt_done pt_ready pv_done o_ready csm_ready a_row a_seg a_exp b_ready y_done state_ready state_out
    yg_ready sqg_ready g_stat g_diag g_val g_hi g_ready z_tanh groups_over
    oa_hi oa_ready pg_k pg_r qb_ready sc_done s_bias s_exp s_prob pn_ready ga_tanh gb_tanh
    olat_hi_s olat_ready ov_hi ov_ready mg_val mg_hi mg_ready
    mix_sq x_again n_stat n_diag x2_val x2_sq h_val h_hi h_ready relu_a f_hi f_ready acc_sq y_val y_out""".split()


def _lay_small():
    at = 0
    for name, n in (("gpre", 8), ("gq", 3), ("gkv", 2), ("gssm", 16), ("gpost", 8), ("gpremlp", 8),
                    ("gpostmlp", 8), ("dskip", 16), ("dtbias", 1), ("alog", 1), ("conv", 8 * 4 * 5)):
        SMALL[name] = (at, n)
        at += n
    return at


N_SMALL = _lay_small()


def build_layer(nc, d, o):
    ctx = ExitStack()
    with ctx:
        def sb(name, shape, dt=F32):
            return ctx.enter_context(nc.sbuf_tensor(name, shape, dt))

        def sem(name):
            return ctx.enter_context(nc.semaphore(name))

        w_stage = sb("w_stage", [P, 2, 1024])
        w_hi = sb("w_hi", [P, 2, 1024], F32R)
        w_lo = sb("w_lo", [P, 2, 1024], F32R)
        act_hi = sb("act_hi", [P, KT, T], F32R)
        act_lo = sb("act_lo", [P, KT, T], F32R)
        mid_hi = sb("mid_hi", [P, KT, T], F32R)
        mid_lo = sb("mid_lo", [P, KT, T], F32R)
        acc = sb("acc", [P, KT, T])
        o_attn = sb("o_attn", [P, KT, SEQ])
        qbd_hi = sb("qbd_hi", [P, 16], F32R)
        qbd_lo = sb("qbd_lo", [P, 16], F32R)
        olat_hi = sb("olat_hi", [P, 256], F32R)
        olat_lo = sb("olat_lo", [P, 256], F32R)
        small = sb("small", [P, N_SMALL])
        ident = sb("ident", [P, P])
        amask = sb("amask", [P, P])
        smask = sb("smask", [P, P])
        ropet = sb("ropet", [P, T])
        ones = sb("ones", [P, P])
        rows = sb("rows", [P, 2, NCH, SSM_HEADS])
        cs3 = sb("cs3", [SSM_HEADS, SEQ + 16])
        csm = sb("csm", [SSM_HEADS, HPG, CHUNK])
        sdm = sb("sdm", [SSM_HEADS, HPG, 16])
        sdec = sb("sdec", [P, 2, 16])
        dtx = sb("dtx", [P, 2, NB])
        ysum = sb("ysum", [P, NB])
        qlat = sb("qlat", [P, 2, NB, HEADS])
        qpe_s = sb("qpe_s", [P, NB, HEADS])
        kpe_s = sb("kpe_s", [P, NB])
        ckv_s = sb("ckv_s", [P, 2, NB])
        qlb = sb("qlb", [P, 2, HEADS])
        qpb = sb("qpb", [P, HEADS])
        olat = sb("olat", [P, 2, NB, HEADS])
        pages = sb("pages", [1, NB * PAGES], I32)
        st = sb("st", [P, 3, 8])
        diag_flat = sb("diag", [P, T])
        diag = diag_flat[:, :].rearrange("p (c t) -> p c t", c=8)
        snb = sb("snb", [P, 3])
        sm = sb("sm", [P, 8])
        sms = sb("sms", [P, 8])
        pnd = sb("pnd", [16, 16])
        pnb = sb("pnb", [P, 16])
        ahead = sb("ahead", [SSM_HEADS, 1])

        arena = sb("arena", [P, ARENA])
        at = [0]

        def part(n, pat=None, **kw):
            v = arena[:, at[0]:at[0] + n]
            at[0] += n
            assert at[0] <= ARENA, at[0]
            return v.rearrange(pat, **kw) if pat else v

        x_sb = part(KT * T, "p (k t) -> p k t", k=KT)
        sq = part(KT * T, "p (k t) -> p k t", k=KT)
        lat = part(5 * T, "p (k t) -> p k t", k=5)
        dtw = part(5 * T, "p (k t) -> p k t", k=5)
        at[0] = 0
        raw = part(4 * RAWW, "p (k t) -> p k t", k=4)
        Kt = part(2 * T, "p (h t) -> p h t", h=2)
        xc = part(4 * CONVW, "p (k t) -> p k t", k=4)
        cacc_flat = part(2 * CONVW)
        cacc = cacc_flat.rearrange("p (k t) -> p k t", k=2)
        sqg = cacc_flat[:, 0:2 * T].rearrange("p (k t) -> p k t", k=2)
        sz = part(2 * T, "p (k t) -> p k t", k=2)
        yT = part(2 * T, "p (k t) -> p k t", k=2)
        state = part(256)
        sT = arena[:, at[0]:at[0] + 1024].rearrange("p (b n) -> p b n", b=NB)
        seg = part(512, "p (h l) -> p h l", h=HPG)
        ecs = part(512, "p (h l) -> p h l", h=HPG)
        rtmp = arena[:, at[0]:at[0] + T]
        Mt = part(512, "p (h l) -> p h l", h=HPG)
        Cx = part(512, "p (h l) -> p h l", h=HPG)
        xdt = part(256)
        xdte = part(256)
        Brow = part(128)
        V = part(512, "p (c v) -> p c v", c=NCH)
        Pq = part(1024, "p (u s) -> p u s", u=2)
        PT = part(512)
        sS = part(2048, "p (t b n) -> p t b n", t=2, b=NB)
        Qt = part(2 * T, "p (h t) -> p h t", h=2)
        at[0] = 0
        kT = part(PAGES * 256, "p (j c) -> p j c", j=PAGES)
        kr = part(PAGES * 256, "p (j c) -> p j c", j=PAGES)
        ropek = part(PAGES * PAGE, "p (j t) -> p j t", j=PAGES)
        Pexp = part(PAST + 4)
        PTs = part(256, "p (j h) -> p j h", j=PAGES)
        sga = part(KT * T, "p (k t) -> p k t", k=KT)
        tg = diag_flat
        at[0] = 0
        x2 = part(KT * T, "p (k t) -> p k t", k=KT)
        etmp = arena[:, at[0]:at[0] + 2 * T].rearrange("p (k t) -> p k t", k=2)
        mix = part(KT * T, "p (k t) -> p k t", k=KT)
        sq2 = part(KT * T, "p (k t) -> p k t", k=KT)
        relu = part(2 * T + 68)[:, 68:].rearrange("p (k t) -> p k t", k=2)

        lin = ctx.enter_context(nc.psum_tensor("lin", [P, 2, 2, 512], F32))
        Pb = ctx.enter_context(nc.psum_tensor("Pb", [P, 4, 512], F32))

        def small_of(name, k=0):
            a, _ = SMALL[name]
            return small[:, bass.ds(k + a, 1)] if not isinstance(k, int) else small[:, a + k:a + k + 1]

        def lin_cols(pl, lo=0, hi=P):
            return lin[lo:hi, pl.slot, :, 0:HALF]

        def cols(ap2d):
            return ap2d.rearrange("p (a b) -> p a b", a=2)

        def at_g(ap3, g):
            if isinstance(g, int):
                return ap3[:, g, :]
            return ap3[:, bass.ds(g, 1), :].rearrange("p a b -> p (a b)")

        def spread(ap2, n):
            p_, a_ = ap2.shape
            return ap2.rearrange("p (a o) -> p a o", o=1).to_broadcast([p_, a_, n])

        def repeat(ap2, n):
            p_, a_ = ap2.shape
            return ap2.rearrange("p (o a) -> p o a", o=1).to_broadcast([p_, n, a_])

        S = {n: sem(n) for n in SEMAPHORES}
        block = ctx.enter_context(nc.Block())

        @block.sync
        def _(sp):
            def load_chunk(n, slot):
                sp.dma_start(w_stage[:, slot, :],
                             d["wall"][bass.ds(n, 1), :, :].rearrange("a p c -> p (a c)") if not isinstance(n, int)
                             else d["wall"][n, :, :]).then_inc(S[f"w_loaded{slot}"], 16)

            def next_chunk(n, slot):
                sp.wait_ge(S["w_split"], n - 1)
                load_chunk(n, slot)

            def stream(first, last):
                pairs = (last - first) // 2
                with sp.Fori(0, pairs) as i:
                    for j in range(2):
                        next_chunk(i * 2 + (first + j), (first + j) % 2)
                if (last - first) % 2:
                    next_chunk(last - 1, (last - 1) % 2)

            for k in range(4):
                sp.dma_start(x_sb[:, 2 * k:2 * k + 2, :], d["xT"][:, 2 * k:2 * k + 2, :]).then_inc(S["x_in"], 16)
            for dst, name in ((small, "small"), (ident, "ident"), (ropet, "ropet"), (amask, "amask"),
                              (smask, "smask"), (pages, "pages")):
                sp.dma_start(dst[:, :], d[name]).then_inc(S["consts_in"], 16)
            load_chunk(0, 0)
            load_chunk(1, 1)
            stream(2, CH_D + 2)

            sp.wait_ge(S["groups_over"], 3)
            for n in ("st_out0", "st_out1", "state_out", "conv_out"):
                sp.wait_ge(S[n], 16 * GROUPS)
            sp.wait_ge(S["kpe_out"], 16)

            def load_keys(b):
                for j in range(PAGES):
                    page = sp.value_load(pages[0:1, bass.ds(b * PAGES + j, 1)], min_val=0, max_val=N_PHYS - 1)
                    sp.dma_start(kT[:, j, :], d["cache"][bass.ds(page, 1), :, 0:256].rearrange("a p c -> p (a c)")
                                 ).then_inc(S["pg_k"], 16)
                    sp.dma_start(ropek[64:96, j, :],
                                 d["rope"][bass.ds(page, 1), :, :].rearrange("a p c -> p (a c)")
                                 ).then_inc(S["pg_k"], 16)

            def load_rows(b):
                for j in range(PAGES):
                    page = sp.value_load(pages[0:1, bass.ds(b * PAGES + j, 1)], min_val=0, max_val=N_PHYS - 1)
                    sp.dma_start(kr[:, j, :], d["cache"][bass.ds(page, 1), :, 256:512].rearrange("a p c -> p (a c)")
                                 ).then_inc(S["pg_r"], 16)

            load_keys(0)
            load_rows(0)
            with sp.Fori(1, NB) as b:
                sp.wait_ge(S["sc_done"], b)
                sp.sem_inc(S["sp_gate"], 1)
                load_keys(b)
                for j in range(2):
                    next_chunk(b * 2 + (CH_D + j), (CH_D + j) % 2)
                sp.wait_ge(S["lin_done"], b * len(ROW_LIN) + LIN_D)
                sp.sem_inc(S["sp_gate"], 1)
                load_rows(b)
            stream(CH_OV, CH_F)
            sp.wait_ge(S["lin_free"], LIN_OV)
            for k in range(4):
                sp.dma_start(x2[:, 2 * k:2 * k + 2, :], d["xT"][:, 2 * k:2 * k + 2, :]).then_inc(S["x_again"], 16)
            stream(CH_F, N_CHUNKS)
            for k in range(KT):
                sp.wait_ge(S["y_val"], k + 1)
                sp.dma_start(o["yT"][:, k, :], mix[:, k, :]).then_inc(S["y_out"], 16)
            sp.wait_ge(S["y_out"], 16 * KT)

        @block.gpsimd
        def _(pool):
            with pool.Fori(0, N_CHUNKS // 2) as i:
                for j in range(2):
                    pool.wait_ge(S["w_hi_done"], i * 2 + (j + 1))
                    pool.tensor_tensor(w_lo[:, j, :], w_stage[:, j, :], w_hi[:, j, :].bitcast(F32), ALU.subtract
                                       ).then_inc(S["w_split"], 1)

        @block.tensor
        def _(pe):
            def free_slot(pl):
                if not isinstance(pl.index, int) or pl.index >= 2:
                    pe.wait_ge(S["lin_free"], pl.index - 1)

            def open_chunk(ch, first_matmul):
                if not isinstance(ch.index, int) or ch.index >= 1:
                    first_matmul.then_inc(S["w_used"], 1)

            def linear(pl, ch, offs, rhs, opens=True):
                if opens:
                    pe.wait_ge(S["w_split"], ch.index + 1)
                free_slot(pl)
                n = len(offs)
                first = True
                for k, (off, (rh, rl)) in enumerate(zip(offs, rhs)):
                    for w, r, p in ((w_hi, rh, 0), (w_hi, rl, 1), (w_lo, rh, 2)):
                        for hf in range(2):
                            mm = pe.matmul(lin[:, pl.slot, hf, 0:HALF], w[:, ch.slot, off:off + P],
                                           r[:, hf * HALF:(hf + 1) * HALF],
                                           start=(k == 0 and p == 0), stop=(k == n - 1 and p == 2))
                            if first and opens:
                                open_chunk(ch, mm)
                            first = False
                mm.then_inc(S["lin_done"], 1)

            def act_rhs(n=KT):
                return [(act_hi[:, k, :], act_lo[:, k, :]) for k in range(n)]

            def mid_rhs(a, n):
                return [(mid_hi[:, k, :], mid_lo[:, k, :]) for k in range(a, a + n)]

            def statistics(out, src, n):
                for c in range(8):
                    for k in range(n):
                        mm = pe.matmul(out[:, c:c + 1], src[:, k, TOKT * c:TOKT * (c + 1)], ones[:, 0:1],
                                       start=(k == 0), stop=(k == n - 1))
                return mm

            def broadcast_stat(pl):
                free_slot(pl)
                for hf in range(2):
                    mm = pe.matmul(lin[:, pl.slot, hf, 0:HALF], ones[0:TOKT, :], diag[0:TOKT, 4 * hf:4 * hf + 4, :],
                                   start=True, stop=True)
                mm.then_inc(S["lin_done"], 1)

            K8 = [k * P for k in range(KT)]
            pe.wait_ge(S["ones_set"], 1)
            pe.wait_ge(S["consts_in"], 16 * 6)
            pe.wait_ge(S["sq_x"], 2)
            statistics(Pb[0:TOKT, 2, 0:8], sq, KT).then_inc(S["stat_done"], 1)
            pe.wait_ge(S["rstd_diag"], 1)
            broadcast_stat(fixed(0))
            pe.wait_ge(S["act_ready"], KT)
            for k in range(6):
                linear(fixed(1 + k), fixed(k), K8, act_rhs())
            pe.wait_ge(S["lat_sq"], 3)
            statistics(Pb[0:TOKT, 2, 8:16], sq[:, 0:3, :], 3).then_inc(S["stat_done"], 1)
            pe.wait_ge(S["lat_sq"], 5)
            statistics(Pb[0:TOKT, 0, 0:8], sq[:, 3:5, :], 2).then_inc(S["stat_done"], 1)
            pe.wait_ge(S["rstd_diag"], 2)
            broadcast_stat(fixed(7))
            pe.wait_ge(S["rstd_diag"], 3)
            broadcast_stat(fixed(8))
            pe.wait_ge(S["cs_ready"], 1)
            for c in range(NCH):
                pe.transpose(Pb[:, 3, 32 * c:32 * c + 32], cs3[:, CHUNK * c:CHUNK * (c + 1)], ident[0:32, 0:32])
            for c in range(NCH):
                tr = pe.transpose(Pb[:, 3, 128 + 32 * c:160 + 32 * c], dtw[0:32, 0, CHUNK * c:CHUNK * (c + 1)],
                                  ident[0:32, 0:32])
            tr.then_inc(S["rows_tr"], 1)

            def group(i):
                has_in = not (isinstance(i, int) and i == GROUPS)
                has_rest = not (isinstance(i, int) and i == 0)
                g = i - 1

                def project(name):
                    if has_in:
                        linear(c_lin(i, name), c_chunk(i, name), K8, act_rhs())

                if not has_rest:
                    for name in IN_LIN:
                        project(name)
                    return

                def scores(u):
                    h, q, pb = u // 4, u % 4, u % 2
                    if u >= 2:
                        pe.wait_ge(S["o_ready"], g * 8 + (u - 1))
                    pe.matmul(Pb[:, pb, 0:(q + 1) * P], Qt[0:96, h, q * P:(q + 1) * P], Kt[0:96, h, 0:(q + 1) * P],
                              start=True, stop=False)
                    pe.matmul(Pb[:, pb, q * P:(q + 1) * P], ident[:, :], amask[:, :],
                              start=False, stop=True).then_inc(S["scores"], 1)

                def transposes(u):
                    q, pb = u % 4, u % 2
                    pe.wait_ge(S["prob_ready"], g * 8 + (u + 1))
                    for j in range(q + 1):
                        tr = pe.transpose(Pb[:, 2, j * P:(j + 1) * P], Pq[:, pb, j * P:(j + 1) * P], ident[:, :])
                    tr.then_inc(S["pt_done"], 1)

                def values(u):
                    h, q, pb = u // 4, u % 4, u % 2
                    pe.wait_ge(S["pt_ready"], g * 8 + (u + 1))
                    for j in range(q + 1):
                        mm = pe.matmul(Pb[64 * h:64 * h + 64, pb, 0:P], V[:, j, 64 * h:64 * h + 64],
                                       PT[:, j * P:(j + 1) * P], start=(j == 0), stop=(j == q))
                    mm.then_inc(S["pv_done"], 1)

                def scan_front(c):
                    pl = c_lin(i, f"sA{c}")
                    free_slot(pl)
                    pe.wait_ge(S["csm_ready"], g * 4 + (c + 1))
                    tok = slice(CHUNK * c, CHUNK * (c + 1))
                    pe.matmul(lin[:, pl.slot, 0, :], ones[0:32, :], csm[:, :, :], start=True, stop=True)
                    for t in range(3):
                        pe.transpose(lin[:, pl.slot, 1, t * P:(t + 1) * P], xc[:, t, tok], ident[:, :])
                    pe.matmul(lin[:, pl.slot, 1, 3 * P:4 * P], xc[:, 2, tok], xc[:, 3, tok],
                              start=True, stop=True).then_inc(S["lin_done"], 1)

                def scan_back(c):
                    pe.wait_ge(S["b_ready"], g * 4 + (c + 1))
                    if c:
                        pe.wait_ge(S["state_ready"], g * 4 + c)
                    for h in range(HPG):
                        out = Pb[64 * (h % 2):64 * (h % 2) + 64, 3, P * (h // 2):P * (h // 2) + P]
                        pe.matmul(out, xdt[:, 64 * h:64 * h + 64], Mt[:, h, :], start=True, stop=(c == 0))
                        if c:
                            pe.matmul(out, state[:, 64 * h:64 * h + 64], Cx[:, h, :], start=False, stop=True)
                    pe.matmul(Pb[:, 3, 256:512], Brow[:, :], xdte[:, :], start=True, stop=True
                              ).then_inc(S["y_done"], 1)

                pe.wait_ge(S["act_ready"], KT + 5)
                for h in range(2):
                    linear(c_lin(i, f"uq{h}"), c_chunk(i, "UQ"), [k * 256 + h * P for k in range(3)], mid_rhs(0, 3),
                           opens=(h == 0))
                ch = c_chunk(i, "UKV")
                linear(c_lin(i, "uk"), ch, [0, P], mid_rhs(3, 2))
                pl = c_lin(i, "uv")
                free_slot(pl)
                for c in range(NCH):
                    for k in range(2):
                        tok = slice(CHUNK * c, CHUNK * (c + 1))
                        a, b = mid_hi[:, 3 + k, tok], mid_lo[:, 3 + k, tok]
                        wh = w_hi[:, ch.slot, 512 + k * P:640 + k * P]
                        wl = w_lo[:, ch.slot, 512 + k * P:640 + k * P]
                        for n, (x, w) in enumerate(((a, wh), (a, wl), (b, wh))):
                            mm = pe.matmul(lin[:, pl.slot, 0, c * P:(c + 1) * P], x, w,
                                           start=(k == 0 and n == 0), stop=(k == 1 and n == 2))
                mm.then_inc(S["lin_done"], 1)
                pl = c_lin(i, "ql")
                free_slot(pl)
                pe.wait_ge(S["lin_free"], c_lin(i, "uq1").index + 1)
                for k in range(2):
                    out = lin[:, pl.slot, 0, 16 * k:16 * k + 16]
                    for n, (w, r) in enumerate(((w_hi, qbd_hi), (w_hi, qbd_lo), (w_lo, qbd_hi))):
                        mm = pe.matmul(out, w[:, ch.slot, 256 + k * P:384 + k * P], r[:, :],
                                       start=(n == 0), stop=(n == 2))
                mm.then_inc(S["lin_done"], 1)
                pe.wait_ge(S["sdm_ready"], g + 1)
                pe.matmul(Pb[:, 3, 0:64], ones[0:32, :], sdm[:, :, :], start=True, stop=True
                          ).then_inc(S["sdec_mm"], 1)
                pe.wait_ge(S["xc_ready"], g * 4 + 4)
                for name, k in (("bB", 2), ("bC", 3)):
                    pl = c_lin(i, name)
                    free_slot(pl)
                    for b in range(NB):
                        mm = pe.matmul(lin[:, pl.slot, b // 4, (b % 4) * P:(b % 4 + 1) * P],
                                       xc[:, k, SAMP0 + 4 * b:SAMP0 + 4 * b + 1].to_broadcast([P, P]), ident[:, :],
                                       start=True, stop=True)
                    mm.then_inc(S["lin_done"], 1)
                pe.wait_ge(S["q_ready"], g * 2 + 2)
                pe.wait_ge(S["lin_free"], c_lin(i, "uv").index + 1)
                scores(0)
                for u in range(8):
                    if u < 7:
                        scores(u + 1)
                    if u % 2 == 0:
                        scan_front(u // 2)
                        project(IN_LIN[u // 2])
                    transposes(u)
                    if u % 2:
                        scan_back(u // 2)
                    values(u)
                pe.wait_ge(S["o_ready"], g * 8 + 8)
                pe.wait_ge(S["sqg_ready"], g + 1)
                statistics(Pb[0:TOKT, 2, 0:8], sqg, 2).then_inc(S["g_stat"], 1)
                project("z0")
                project("z1")
                pe.wait_ge(S["g_diag"], g + 1)
                broadcast_stat(c_lin(i, "bc"))
                pe.wait_ge(S["g_ready"], g * 2 + 2)
                for m in range(8):
                    linear(c_lin(i, f"s{m}"), c_chunk(i, "SA" if m < 4 else "SB"),
                           [(m % 4) * P, 512 + (m % 4) * P], mid_rhs(5, 2), opens=(m % 4 == 0))

            group(0)
            with pe.Fori(1, GROUPS) as i:
                group(i)
            group(GROUPS)
            pe.drain().then_inc(S["groups_over"], 1)

            per = len(ROW_LIN)
            with pe.Fori(0, NB) as b:
                def pl_of(name):
                    return looped(LIN_D, per, b, ROW_LIN.index(name))
                pe.wait_ge(S["qb_ready"], b + 1)
                pl = pl_of("SN")
                free_slot(pl)
                for k in range(2):
                    pe.matmul(lin[0:16, pl.slot, 0, 0:1], qlb[:, k, :], snb[:, k:k + 1], start=(k == 0), stop=False)
                pe.matmul(lin[0:16, pl.slot, 0, 0:1], qpb[64:96, :], snb[64:96, 2:3], start=False, stop=True
                          ).then_inc(S["lin_done"], 1)
                pe.wait_ge(S["pg_k"], b * (32 * PAGES) + 32 * PAGES)
                for n in range(4):
                    for k in range(2):
                        pe.matmul(Pb[0:16, n, :], qlb[:, k, :], kT[:, 4 * n:4 * n + 4, k * P:(k + 1) * P],
                                  start=(k == 0), stop=False)
                    mm = pe.matmul(Pb[0:16, n, :], qpb[64:96, :], ropek[64:96, 4 * n:4 * n + 4, :],
                                   start=False, stop=True)
                mm.then_inc(S["sc_done"], 1)
                for j, name in enumerate(("ga", "gb")):
                    linear(pl_of(name), looped(CH_D, 2, b, j), K8, act_rhs())
                pl = pl_of("PT")
                free_slot(pl)
                pe.wait_ge(S["s_prob"], b + 1)
                pe.sem_inc(S["pe_gate"], 1)
                for j in range(PAGES):
                    tr = pe.transpose(lin[:, pl.slot, 0, 16 * j:16 * j + 16], Pexp[0:16, j * P:(j + 1) * P],
                                      ident[0:16, 0:16])
                tr.then_inc(S["lin_done"], 1)
                pl = pl_of("PN")
                free_slot(pl)
                pe.wait_ge(S["pn_ready"], b + 1)
                pe.matmul(lin[:, pl.slot, 0, 0:16], ones[0:16, :], pnd[:, :], start=True, stop=True
                          ).then_inc(S["lin_done"], 1)
                pl = pl_of("OL")
                pe.wait_ge(S["lin_free"], pl_of("PT").index + 1)
                pe.wait_ge(S["pg_r"], b * (16 * PAGES) + 16 * PAGES)
                for k in range(2):
                    for j in range(PAGES):
                        mm = pe.matmul(lin[:, pl.slot, k, 0:16], kr[:, j, k * P:(k + 1) * P], PTs[:, j, :],
                                       start=(j == 0), stop=(j == PAGES - 1))
                mm.then_inc(S["lin_done"], 1)

            pl = fixed(LIN_OV)
            free_slot(pl)
            pe.wait_ge(S["olat_ready"], 1)
            for pr in range(8):
                ch = fixed(CH_OV + pr // 4)
                if pr % 4 == 0:
                    pe.wait_ge(S["w_split"], ch.index + 1)
                for k in range(2):
                    off = (pr % 4) * 256 + k * P
                    view = [x[:, k * P:(k + 1) * P].rearrange("p (b h) -> p b h", b=NB)[:, :, 2 * pr:2 * pr + 2]
                            for x in (olat_hi, olat_lo)]
                    for n, (w, r) in enumerate(((w_hi, view[0]), (w_hi, view[1]), (w_lo, view[0]))):
                        mm = pe.matmul(lin[:, pl.slot, 0, 16 * pr:16 * pr + 16], w[:, ch.slot, off:off + P], r,
                                       start=(k == 0 and n == 0), stop=(k == 1 and n == 2))
                        if pr % 4 == 0 and k == 0 and n == 0:
                            open_chunk(ch, mm)
            mm.then_inc(S["lin_done"], 1)

            pe.wait_ge(S["oa_ready"], KT)
            pe.wait_ge(S["ov_ready"], 2)
            with pe.Fori(0, KT // 2) as i:
                for j in range(2):
                    linear(looped(LIN_E, 2, i, j), looped(CH_E, 2, i, j), K8, mid_rhs(0, KT))
            pe.wait_ge(S["mg_ready"], KT)
            with pe.Fori(0, KT // 2) as i:
                for j in range(2):
                    linear(looped(LIN_F, 2, i, j), looped(CH_F, 2, i, j), K8, act_rhs())
            pe.wait_ge(S["mix_sq"], KT)
            statistics(Pb[0:TOKT, 0, 0:8], sq2, KT).then_inc(S["n_stat"], 1)
            pe.wait_ge(S["n_diag"], 1)
            broadcast_stat(fixed(LIN_N))
            pe.wait_ge(S["x2_sq"], KT)
            statistics(Pb[0:TOKT, 0, 8:16], sq2, KT).then_inc(S["n_stat"], 1)
            pe.wait_ge(S["n_diag"], 2)
            broadcast_stat(fixed(LIN_N + 1))
            pe.wait_ge(S["h_ready"], KT)

            def up(lin_at, ch_at):
                for j in range(4):
                    linear(lin_at(j), ch_at(j), K8, act_rhs())

            def down(lin_at, ch_at, blk_slot, blk):
                pe.wait_ge(S["f_ready"], blk * 4 + 4)
                for m in range(8):
                    linear(lin_at(m), ch_at(m // 2), [k * 256 + (m % 2) * P for k in range(4)],
                           mid_rhs(4 * blk_slot, 4), opens=(m % 2 == 0))

            up(lambda j: fixed(LIN_G + j), lambda j: fixed(CH_G + j))
            with pe.Fori(0, 3) as i:
                for j in range(2):
                    la, ca = LIN_G + 4 + 12 * j, CH_G + 4 + 8 * j
                    up(lambda k: looped(la, 24, i, k), lambda k: looped(ca, 16, i, k))
                    down(lambda k: looped(la + 4, 24, i, k), lambda k: looped(ca + 4, 16, i, k), j, i * 2 + j)
            la, ca = LIN_G + 4 + 72, CH_G + 4 + 48
            up(lambda k: fixed(la + k), lambda k: fixed(ca + k))
            down(lambda k: fixed(la + 4 + k), lambda k: fixed(ca + 4 + k), 0, 6)
            down(lambda k: fixed(la + 12 + k), lambda k: fixed(ca + 8 + k), 1, 7)
            pe.wait_ge(S["acc_sq"], KT)
            statistics(Pb[0:TOKT, 0, 0:8], sq2, KT).then_inc(S["n_stat"], 1)
            pe.wait_ge(S["n_diag"], 3)
            broadcast_stat(fixed(LIN_H))

        @block.scalar
        def _(act):
            chain = Chain(act, S["act_chain"])

            def done(pl):
                act.wait_ge(S["lin_done"], pl.index + 1)

            def round_chunk(ch):
                act.wait_ge(S[f"w_loaded{ch.slot}"], ch.turn * 16 + 16)
                if not (isinstance(ch.index, int) and ch.index < 2):
                    act.wait_ge(S["w_used"], ch.index - 1)
                act.activation(w_hi[:, ch.slot, :], w_stage[:, ch.slot, :], ACT.Copy).then_inc(S["w_hi_done"], 1)

            for k in range(2):
                act.wait_ge(S["x_in"], 16 * 4)
                act.activation(sq[:, 4 * k:4 * k + 4, :], x_sb[:, 4 * k:4 * k + 4, :], ACT.Square
                               ).then_inc(S["sq_x"], 1)
            act.wait_ge(S["consts_in"], 16 * 6)
            act.activation(ahead[:, :], small_of("alog")[0:32, :], ACT.Exp).then_inc(S["exp_alog"], 1)
            round_chunk(fixed(0))
            for k in range(KT):
                act.wait_ge(S["norm_val"], k + 1)
                act.activation(act_hi[:, k, :], sq[:, k, :], ACT.Copy).then_inc(S["norm_hi"], 1)
            round_chunk(fixed(1))
            done(fixed(1))
            act.activation(cols(dtw[0:32, 0, :]), lin_cols(fixed(1), 0, 32), ACT.Identity,
                           bias=small_of("dtbias")[0:32, :]).then_inc(S["dt_raw"], 1)
            for k in range(5):
                round_chunk(fixed(2 + k))
                done(fixed(2 + k))
                act.activation(cols(sq[:, k, :]), lin_cols(fixed(2 + k)), ACT.Square).then_inc(S["lat_sq"], 1)
            chain.link(act.activation(dtw[0:32, 1, :], dtw[0:32, 0, :], ACT.Abs))
            chain.link(act.activation(dtw[0:32, 1, :], dtw[0:32, 1, :], ACT.Exp, scale=-1.0))
            act.activation(dtw[0:32, 3, :], dtw[0:32, 1, :], ACT.Ln, bias=1.0).then_inc(S["sp_ln"], 1)
            for k in range(5):
                act.wait_ge(S["norm_val"], KT + k + 1)
                act.activation(mid_hi[:, k, :], sq[:, k, :], ACT.Copy).then_inc(S["norm_hi"], 1)
            act.dma_start(o["kvT"], sq[:, 3:5, :]).then_inc(S["kv_out"], 16)
            act.dma_start(o["kpeT"], Kt[64:96, 0, :]).then_inc(S["kpe_out"], 16)
            act.wait_ge(S["cs_ready"], 1)
            act.activation(cs3[:, SEQ + 8:SEQ + 16], dtw[0:32, 0, SEQ:T], ACT.Exp, scale=ahead[:, :]
                           ).then_inc(S["sp_ln"], 1)
            act.wait_ge(S["kv_out"], 16)
            act.wait_ge(S["rows_ready"], 1)

            def group(i):
                has_in = not (isinstance(i, int) and i == GROUPS)
                has_rest = not (isinstance(i, int) and i == 0)
                g = i - 1
                hist = d["hist"]
                if has_in:
                    if has_rest:
                        act.wait_ge(S["xc_ready"], i * 4)
                        act.wait_ge(S["conv_out"], i * 16)
                        act.dma_start(raw[:, :, SAMP0:RAWW],
                                      hist[bass.ds(i, 1)].rearrange("a p k c -> p (a k) c")).then_inc(S["hist_in"], 16)
                    else:
                        act.dma_start(raw[:, :, SAMP0:RAWW], hist[0]).then_inc(S["hist_in"], 16)

                def raw_evac(k):
                    if has_in:
                        pl = c_lin(i, IN_LIN[k])
                        round_chunk(c_chunk(i, IN_LIN[k]).next())
                        done(pl)
                        act.activation(raw[:, k, 3:3 + HALF], lin[:, pl.slot, 0, 0:HALF], ACT.Copy)
                        act.activation(raw[:, k, 3 + HALF:3 + SEQ], lin[:, pl.slot, 1, 0:SEQ - HALF], ACT.Copy
                                       ).then_inc(S["raw_act"], 1)

                def z_evac():
                    for k in range(2):
                        pl = c_lin(i, f"z{k}")
                        round_chunk(c_chunk(i, f"z{k}").next())
                        done(pl)
                        act.activation(cols(sz[:, k, :]), lin_cols(pl), ACT.Tanh, scale=0.5
                                       ).then_inc(S["z_tanh"], 1)

                def finish_inputs():
                    for k in range(4):
                        act.wait_ge(S["conv_acc"], i * 4 + (k + 1))
                        act.activation(xc[:, k, :], cacc[:, k % 2, :], ACT.Tanh).then_inc(S["conv_tanh"], 1)
                        if has_rest and k == 1:
                            round_chunk(c_chunk(i, "SB").next())
                    act.wait_ge(S["lin_free"], c_lin(i, "c").index + 1)
                    act.dma_start(o["convT"][bass.ds(i, 1)].rearrange("a p k c -> p (a k) c") if has_rest
                                  else o["convT"][0], raw[:, :, SEQ:RAWW]).then_inc(S["conv_out"], 16)
                    for t in range(2):
                        if has_rest:
                            act.wait_ge(S[f"st_out{t}"], i * 16)
                        src = d["state"][:, bass.ds(i * 4 + 2 * t, 2), :, :] if has_rest \
                            else d["state"][:, 2 * t:2 * t + 2, :, :]
                        act.dma_start(sS[:, t], src.rearrange("b h p n -> (h p) b n")).then_inc(S[f"st_in{t}"], 16)

                if not has_rest:
                    for k in range(4):
                        raw_evac(k)
                    z_evac()
                    finish_inputs()
                    return

                def exponent(u):
                    q, pb = u % 4, u % 2
                    act.wait_ge(S["max_bias"], g * 8 + (u + 1))
                    act.activation(Pq[:, pb, 0:(q + 1) * P], Pb[:, pb, 0:(q + 1) * P], ACT.Exp,
                                   bias=sm[:, 2 + pb:3 + pb], scale=SM_SCALE, accum_out=sm[:, 4 + pb:5 + pb]
                                   ).then_inc(S["exp_done"], 1)

                round_chunk(c_chunk(i, "UKV"))
                for h in range(2):
                    pl = c_lin(i, f"uq{h}")
                    done(pl)
                    act.activation(cols(Qt[0:64, h, :]), lin_cols(pl, 0, 64), ACT.Copy)
                    act.activation(qbd_hi[64 * h:64 * h + 64, 8 * h:8 * h + 8], lin[0:64, pl.slot, 1, HALF - NB:HALF],
                                   ACT.Copy).then_inc(S["qbd_hi_s"], 1)
                pl = c_lin(i, "uk")
                round_chunk(c_chunk(i, "UKV").next())
                done(pl)
                act.activation(cols(Kt[0:64, 0, :]), lin_cols(pl, 0, 64), ACT.Copy).then_inc(S["k_act"], 1)
                pl = c_lin(i, "uv")
                done(pl)
                act.activation(V[:, 0:2, :], lin[:, pl.slot, 0, 0:256].rearrange("p (c v) -> p c v", c=2), ACT.Copy
                               ).then_inc(S["v_act"], 1)
                exponent(0)
                for u in range(8):
                    h, q, pb = u // 4, u % 4, u % 2
                    if u < 7:
                        exponent(u + 1)
                    if u % 2 == 0:
                        c = u // 2
                        pl = c_lin(i, f"sA{c}")
                        done(pl)
                        if c:
                            act.wait_ge(S["state_ready"], g * 4 + c)
                        act.activation(Brow[:, :], lin[:, pl.slot, 1, 256:384], ACT.Copy).then_inc(S["a_row"], 1)
                        act.wait_ge(S["a_seg"], g * 4 + (c + 1))
                        act.activation(ecs[:, :, :], lin[:, pl.slot, 0, :].rearrange("p (h l) -> p h l", h=HPG),
                                       ACT.Exp)
                        act.activation(seg[:, :, :], seg[:, :, :], ACT.Exp).then_inc(S["a_exp"], 1)
                        raw_evac(c)
                    act.wait_ge(S["pt_done"], g * 8 + (u + 1))
                    act.activation(PT[:, 0:(q + 1) * P], Pb[:, 2, 0:(q + 1) * P], ACT.Copy).then_inc(S["pt_ready"], 1)
                    act.wait_ge(S["pv_done"], g * 8 + (u + 1))
                    act.activation(at_g(o_attn[64 * h:64 * h + 64], g)[:, q * P:(q + 1) * P],
                                   Pb[64 * h:64 * h + 64, pb, 0:P], ACT.Copy).then_inc(S["o_ready"], 1)
                    if u == 1:
                        for t in range(2):
                            act.wait_ge(S["st_new"], g * 2 + (t + 1))
                            act.dma_start(o["stateT"][:, bass.ds(g * 4 + 2 * t, 2), :, :].rearrange(
                                "b h p n -> (h p) b n"), sS[:, t]).then_inc(S[f"st_out{t}"], 16)
                act.wait_ge(S["state_ready"], g * 4 + 4)
                act.dma_start(o["ssmT"][bass.ds(g, 1)].rearrange("a p c -> p (a c)"), state[:, :]
                              ).then_inc(S["state_out"], 16)
                act.wait_ge(S["yg_ready"], g + 1)
                act.activation(sqg[:, :, :], yT[:, :, :], ACT.Square).then_inc(S["sqg_ready"], 1)
                if has_in:
                    z_evac()
                for t in range(2):
                    act.wait_ge(S["g_val"], g * 2 + (t + 1))
                    act.activation(mid_hi[:, 5 + t, :], yT[:, t, :], ACT.Copy).then_inc(S["g_hi"], 1)
                round_chunk(c_chunk(i, "SB"))
                if has_in:
                    finish_inputs()
                else:
                    round_chunk(c_chunk(i, "SB").next())

            group(0)
            with act.Fori(1, GROUPS) as i:
                group(i)
            group(GROUPS)
            act.drain().then_inc(S["groups_over"], 1)

            for k in range(KT):
                act.wait_ge(S["lin_done"], LIN_D)
                act.activation(mid_hi[:, k, 0:SEQ], o_attn[:, k, :], ACT.Copy).then_inc(S["oa_hi"], 1)
            per = len(ROW_LIN)
            with act.Fori(0, NB) as b:
                def pl_of(name):
                    return looped(LIN_D, per, b, ROW_LIN.index(name))
                round_chunk(looped(CH_D, 2, b, 1))
                act.wait_ge(S["s_bias"], b + 1)
                act.activation(Pexp[0:16, 0:PAST], Pb[0:16, :, :].rearrange("p a b -> p (a b)"), ACT.Exp,
                               bias=sms[0:16, 2:3], scale=SM_SCALE, accum_out=sms[0:16, 3:4])
                act.activation(Pexp[0:16, PAST:PAST + 1], Pexp[0:16, PAST:PAST + 1], ACT.Exp,
                               bias=sms[0:16, 2:3], scale=SM_SCALE).then_inc(S["s_exp"], 1)
                done(pl_of("ga"))
                act.activation(cols(at_g(sga, b)), lin_cols(pl_of("ga")), ACT.Tanh, scale=0.5
                               ).then_inc(S["ga_tanh"], 1)
                round_chunk(looped(CH_D, 2, b, 2))
                done(pl_of("gb"))
                act.activation(cols(tg[:, :]), lin_cols(pl_of("gb")), ACT.Tanh, scale=0.5).then_inc(S["gb_tanh"], 1)
            act.wait_ge(S["lin_free"], LIN_OV)
            act.activation(olat_hi[:, :], olat[:, :, :, :].rearrange("p k b h -> p (k b h)"), ACT.Copy
                           ).then_inc(S["olat_hi_s"], 1)
            round_chunk(fixed(CH_OV + 1))
            round_chunk(fixed(CH_E))
            done(fixed(LIN_OV))
            for h in range(2):
                src = lin[64 * h:64 * h + 64, LIN_OV % 2, 0, 0:128].rearrange("p (k b h) -> p k b h", k=8, h=2)
                act.activation(mid_hi[64 * h:64 * h + 64, :, SEQ:T], src[:, :, :, h], ACT.Copy).then_inc(S["ov_hi"], 1)
            with act.Fori(0, KT // 2) as i:
                for j in range(2):
                    round_chunk(looped(CH_E, 2, i, j + 1))
                    act.wait_ge(S["mg_val"], i * 2 + (j + 1))
                    act.activation(at_g(act_hi, i * 2 + j), etmp[:, j, :], ACT.Copy).then_inc(S["mg_hi"], 1)
            with act.Fori(0, KT // 2) as i:
                for j in range(2):
                    pl = looped(LIN_F, 2, i, j)
                    round_chunk(looped(CH_F, 2, i, j + 1))
                    done(pl)
                    act.activation(cols(at_g(sq2, i * 2 + j)), lin_cols(pl), ACT.Square).then_inc(S["mix_sq"], 1)
            for k in range(KT):
                act.wait_ge(S["x2_val"], k + 1)
                act.activation(sq2[:, k, :], x2[:, k, :], ACT.Square).then_inc(S["x2_sq"], 1)
            for k in range(KT):
                act.wait_ge(S["h_val"], k + 1)
                act.activation(act_hi[:, k, :], mix[:, k, :], ACT.Copy).then_inc(S["h_hi"], 1)

            def up(lin_at, ch_at, blk_slot):
                for j in range(4):
                    pl = lin_at(j)
                    round_chunk(ch_at(j + 1))
                    done(pl)
                    act.activation(cols(relu[:, j % 2, :]), lin_cols(pl), ACT.Relu).then_inc(S["relu_a"], 1)
                    act.wait_ge(S["lin_free"], pl.index + 1)
                    act.activation(mid_hi[:, 4 * blk_slot + j, :], relu[:, j % 2, :], ACT.Copy
                                   ).then_inc(S["f_hi"], 1)

            def down(ch_at, n=4):
                for j in range(n):
                    round_chunk(ch_at(j + 1))

            up(lambda j: fixed(LIN_G + j), lambda j: fixed(CH_G + j), 0)
            with act.Fori(0, 3) as i:
                for j in range(2):
                    la, ca = LIN_G + 4 + 12 * j, CH_G + 4 + 8 * j
                    up(lambda k: looped(la, 24, i, k), lambda k: looped(ca, 16, i, k), 1 - j)
                    down(lambda k: looped(ca + 4, 16, i, k))
            ca = CH_G + 4 + 48
            up(lambda k: fixed(LIN_G + 76 + k), lambda k: fixed(ca + k), 1)
            down(lambda k: fixed(ca + 4 + k))
            down(lambda k: fixed(ca + 8 + k), 3)
            act.wait_ge(S["lin_free"], LIN_H)
            for k in range(KT):
                act.activation(sq2[:, k, :], acc[:, k, :], ACT.Square).then_inc(S["acc_sq"], 1)

        @block.vector
        def _(dve):
            chain = Chain(dve, S["dve_chain"])
            link = chain.link

            def done(pl):
                dve.wait_ge(S["lin_done"], pl.index + 1)

            def inverse_rms(src, mean_scale, signal):
                ms, y, t = st[0:TOKT, 0, :], st[0:TOKT, 1, :], st[0:TOKT, 2, :]
                link(dve.tensor_scalar(ms, src, mean_scale, EPS, ALU.mult, ALU.add))
                link(dve.tensor_single_scalar(y.bitcast(I32), ms.bitcast(I32), 1, ALU.logical_shift_right))
                link(dve.tensor_scalar(y.bitcast(I32), y.bitcast(I32), -1.0, float(0x5f3759df), ALU.mult, ALU.add))
                for _ in range(3):
                    link(dve.tensor_tensor(t, y, y, ALU.mult))
                    link(dve.scalar_tensor_tensor(t, t, -0.5, ms, ALU.mult, ALU.mult))
                    link(dve.scalar_tensor_tensor(y, t, 1.5, y, ALU.add, ALU.mult))
                dve.tensor_tensor(diag[0:TOKT], repeat(ident[0:TOKT, 0:TOKT], 8), spread(y, TOKT), ALU.mult
                                  ).then_inc(signal, 1)

            def normed(n, src, gain, pl, val, hi_of, lo_of, s_val, s_hi, s_ready, base):
                done(pl)

                def low(k):
                    dve.wait_ge(s_hi, base + k + 1)
                    dve.tensor_tensor(lo_of(k), val(k), hi_of(k).bitcast(F32), ALU.subtract).then_inc(s_ready, 1)
                for k in range(n):
                    dve.scalar_tensor_tensor(cols(val(k)), cols(src(k)), gain(k), lin_cols(pl), ALU.mult, ALU.mult
                                             ).then_inc(s_val, 1)
                    if k:
                        low(k - 1)
                low(n - 1)
                dve.nop().then_inc(S["lin_free"], 1)

            dve.memset(ones[:, :], 1.0).then_inc(S["ones_set"], 1)
            dve.memset(qbd_hi[:, :].bitcast(F32), 0.0)
            dve.memset(qbd_lo[:, :].bitcast(F32), 0.0)
            dve.memset(acc[:, :, :], 0.0)
            dve.wait_ge(S["consts_in"], 16 * 6)
            for name in ("conv", "gssm", "gpost"):
                a, n = SMALL[name]
                link(dve.tensor_scalar(small[:, a:a + n], small[:, a:a + n], 0.5, None, ALU.mult))
            dve.wait_ge(S["exp_alog"], 1)
            link(dve.tensor_scalar(ahead[:, :], ahead[:, :], -1.0, None, ALU.mult))
            dve.wait_ge(S["stat_done"], 1)
            inverse_rms(Pb[0:TOKT, 2, 0:8], 1.0 / D_MODEL, S["rstd_diag"])
            normed(KT, lambda k: x_sb[:, k, :], lambda k: small_of("gpre", k), fixed(0), lambda k: sq[:, k, :],
                   lambda k: act_hi[:, k, :], lambda k: act_lo[:, k, :],
                   S["norm_val"], S["norm_hi"], S["act_ready"], 0)
            done(fixed(1))
            link(dve.tensor_tensor(cols(x_sb[64:96, 7, :]), lin_cols(fixed(1), 96, 128), cols(ropet[96:128, :]), ALU.mult))
            link(dve.tensor_tensor(cols(Kt[64:96, 0, :]), lin_cols(fixed(1), 64, 96), cols(ropet[64:96, :]), ALU.mult))
            link(dve.tensor_tensor(Kt[64:96, 0, :], Kt[64:96, 0, :], x_sb[64:96, 7, :], ALU.add))
            dve.tensor_copy(Kt[64:96, 1, :], Kt[64:96, 0, :])
            dve.wait_ge(S["dt_raw"], 1)
            dve.tensor_copy(kpe_s[64:96, :], Kt[64:96, 0, SEQ:T]).then_inc(S["lin_free"], 1)
            for k in range(5):
                done(fixed(2 + k))
                dve.wait_ge(S["lat_sq"], k + 1)
                dve.tensor_copy(cols(lat[:, k, :]), lin_cols(fixed(2 + k))).then_inc(S["lin_free"], 1)
            dve.wait_ge(S["stat_done"], 2)
            inverse_rms(Pb[0:TOKT, 2, 8:16], 1.0 / Q_LORA, S["rstd_diag"])
            normed(3, lambda k: lat[:, k, :], lambda k: small_of("gq", k), fixed(7), lambda k: sq[:, k, :],
                   lambda k: mid_hi[:, k, :], lambda k: mid_lo[:, k, :],
                   S["norm_val"], S["norm_hi"], S["act_ready"], KT)
            dve.wait_ge(S["stat_done"], 3)
            inverse_rms(Pb[0:TOKT, 0, 0:8], 1.0 / KV_LORA, S["rstd_diag"])
            normed(2, lambda k: lat[:, 3 + k, :], lambda k: small_of("gkv", k), fixed(8), lambda k: sq[:, 3 + k, :],
                   lambda k: mid_hi[:, 3 + k, :], lambda k: mid_lo[:, 3 + k, :],
                   S["norm_val"], S["norm_hi"], S["act_ready"], KT + 3)
            dve.tensor_copy(ckv_s[:, :, :], sq[:, 3:5, SEQ:T])
            dve.wait_ge(S["sp_ln"], 1)
            x_, e_, u_, l_, m_ = [dtw[0:32, k, :] for k in range(5)]
            link(dve.tensor_scalar(u_, e_, 1.0, -1.0, ALU.add, ALU.add))
            link(dve.tensor_scalar(m_, u_, 0.0, None, ALU.is_equal))
            link(dve.tensor_tensor(u_, u_, m_, ALU.add))
            link(dve.tensor_tensor(l_, l_, m_, ALU.add))
            link(dve.reciprocal(u_, u_))
            link(dve.tensor_tensor(l_, l_, u_, ALU.mult))
            link(dve.tensor_tensor(l_, l_, e_, ALU.mult))
            link(dve.scalar_tensor_tensor(x_, x_, 0.0, l_, ALU.max, ALU.add))
            link(dve.tensor_scalar(u_[:, 0:SEQ], x_[:, 0:SEQ], ahead[:, :], None, ALU.mult))
            dve.memset(m_[:, 0:CHUNK], 1.0)
            link(dve.tensor_copy(cs3[:, SEQ:SEQ + NB], x_[:, SEQ:T]))
            for c in range(NCH):
                last = dve.tensor_tensor_scan(cs3[:, CHUNK * c:CHUNK * (c + 1)], m_[:, 0:CHUNK],
                                              u_[:, CHUNK * c:CHUNK * (c + 1)], 0.0, ALU.mult, ALU.add)
            last.then_inc(S["cs_ready"], 1)
            dve.wait_ge(S["rows_tr"], 1)
            dve.tensor_copy(rows[:, :, :, :].rearrange("p a c h -> p (a c h)"), Pb[:, 3, 0:256]
                            ).then_inc(S["rows_ready"], 1)
            dve.wait_ge(S["sp_ln"], 2)
            dve.wait_ge(S["rows_ready"], 1)
            dve.wait_ge(S["norm_hi"], KT + 5)
            link(dve.memset(raw[:, :, 0:3], 0.0))

            def group(i):
                has_in = not (isinstance(i, int) and i == GROUPS)
                has_rest = not (isinstance(i, int) and i == 0)
                g = i - 1

                def raw_samples(k):
                    if has_in:
                        pl = c_lin(i, IN_LIN[k])
                        done(pl)
                        if k == 0:
                            dve.wait_ge(S["hist_in"], i * 16 + 16)
                        dve.wait_ge(S["raw_act"], i * 4 + (k + 1))
                        dve.tensor_copy(raw[:, k, SAMP0 + 3:RAWW:4], lin[:, pl.slot, 1, HALF - NB:HALF]
                                        ).then_inc(S["lin_free"], 1)

                def z_gate():
                    for k in range(2):
                        dve.wait_ge(S["z_tanh"], i * 2 + (k + 1))
                        pl = c_lin(i, f"z{k}")
                        dve.scalar_tensor_tensor(cols(sz[:, k, :]), cols(sz[:, k, :]), 1.0, lin_cols(pl),
                                                 ALU.add, ALU.mult).then_inc(S["lin_free"], 1)

                def conv(k):
                    def tap(n):
                        return small_of("conv", i * 20 + (5 * k + n))
                    if k == 0:
                        dve.wait_ge(S["lin_free"], c_lin(i, "c").index + 1)
                    if k >= 2:
                        dve.wait_ge(S["xc_ready"], i * 4 + (k - 1))
                    a = cacc[:, k % 2, :]
                    link(dve.tensor_scalar(a, raw[:, k, 0:CONVW], tap(0), tap(4), ALU.mult, ALU.add))
                    for n in range(1, 3):
                        link(dve.scalar_tensor_tensor(a, raw[:, k, n:n + CONVW], tap(n), a, ALU.mult, ALU.add))
                    dve.scalar_tensor_tensor(a, raw[:, k, 3:3 + CONVW], tap(3), a, ALU.mult, ALU.add
                                             ).then_inc(S["conv_acc"], 1)

                def silu(k):
                    dve.wait_ge(S["conv_tanh"], i * 4 + (k + 1))
                    dve.scalar_tensor_tensor(xc[:, k, :], xc[:, k, :], 1.0, cacc[:, k % 2, :], ALU.add, ALU.mult
                                             ).then_inc(S["xc_ready"], 1)

                if not has_rest:
                    for k in range(4):
                        raw_samples(k)
                    z_gate()
                    for k in range(4):
                        if k:
                            silu(k - 1)
                        conv(k)
                    silu(3)
                    return

                onehot = ident[0:32, bass.ds(g * 4, 4)]

                def masked_decay(c):
                    dve.tensor_tensor(csm[:, :, :], repeat(cs3[:, CHUNK * c:CHUNK * (c + 1)], HPG),
                                      spread(onehot, CHUNK), ALU.mult).then_inc(S["csm_ready"], 1)

                def row_max(u):
                    q, pb = u % 4, u % 2
                    dve.wait_ge(S["scores"], g * 8 + (u + 1))
                    link(dve.reduce_max(sm[:, pb:pb + 1], Pb[:, pb, 0:(q + 1) * P], AX.X))
                    dve.tensor_scalar(sm[:, 2 + pb:3 + pb], sm[:, pb:pb + 1], -SM_SCALE, None, ALU.mult
                                      ).then_inc(S["max_bias"], 1)

                def normalise(u):
                    q, pb = u % 4, u % 2
                    dve.wait_ge(S["exp_done"], g * 8 + (u + 1))
                    link(dve.reciprocal(sm[:, 6 + pb:7 + pb], sm[:, 4 + pb:5 + pb]))
                    dve.tensor_scalar(Pq[:, pb, 0:(q + 1) * P], Pq[:, pb, 0:(q + 1) * P], sm[:, 6 + pb:7 + pb],
                                      None, ALU.mult).then_inc(S["prob_ready"], 1)

                def scan_front(c):
                    pl = c_lin(i, f"sA{c}")
                    done(pl)
                    tok = slice(CHUNK * c, CHUNK * (c + 1))
                    heads = bass.ds(g * 4, 4)
                    link(dve.tensor_tensor(seg[:, :, :], lin[:, pl.slot, 0, :].rearrange("p (h l) -> p h l", h=HPG),
                                           spread(rows[:, 0, c, heads], CHUNK), ALU.subtract))
                    dve.tensor_tensor(seg[:, :, :], seg[:, :, :], repeat(smask[:, :], HPG), ALU.min
                                      ).then_inc(S["a_seg"], 1)
                    dve.wait_ge(S["a_row"], g * 4 + (c + 1))
                    link(dve.tensor_tensor(xdt[:, :].rearrange("p (h d) -> p h d", h=HPG),
                                           lin[:, pl.slot, 1, 0:256].rearrange("p (h d) -> p h d", h=HPG),
                                           spread(rows[:, 1, c, heads], 64), ALU.mult))
                    dve.wait_ge(S["a_exp"], g * 4 + (c + 1))
                    dve.tensor_tensor(xdte[:, :].rearrange("p (h d) -> p h d", h=HPG),
                                      xdt[:, :].rearrange("p (h d) -> p h d", h=HPG),
                                      seg[:, :, CHUNK - 1:CHUNK].to_broadcast([P, HPG, 64]), ALU.mult)
                    dve.tensor_tensor(Mt[:, :, :], repeat(lin[:, pl.slot, 1, 384:512], HPG), seg[:, :, :], ALU.mult
                                      ).then_inc(S["lin_free"], 1)
                    dve.tensor_tensor(Cx[:, :, :], ecs[:, :, :], repeat(xc[:, 3, tok], HPG), ALU.mult
                                      ).then_inc(S["b_ready"], 1)
                    if c < NCH - 1:
                        masked_decay(c + 1)

                def scan_back(c):
                    dve.wait_ge(S["y_done"], g * 4 + (c + 1))
                    for t in range(2):
                        y = dve.scalar_tensor_tensor(yT[:, t, CHUNK * c:CHUNK * (c + 1)],
                                                     xc[:, t, CHUNK * c:CHUNK * (c + 1)], small_of("dskip", g * 2 + t),
                                                     Pb[:, 3, P * t:P * (t + 1)], ALU.mult, ALU.add)
                    if c == 0:
                        dve.tensor_copy(state[:, :], Pb[:, 3, 256:512]).then_inc(S["state_ready"], 1)
                        dve.wait_ge(S["state_ready"], g * 4 + 1)
                        return
                    link(dve.tensor_tensor(state[:, :].rearrange("p (h d) -> p h d", h=HPG),
                                           state[:, :].rearrange("p (h d) -> p h d", h=HPG),
                                           ecs[:, :, CHUNK - 1:CHUNK].to_broadcast([P, HPG, 64]), ALU.mult))
                    dve.tensor_tensor(state[:, :], state[:, :], Pb[:, 3, 256:512], ALU.add
                                      ).then_inc(S["state_ready"], 1)
                    dve.wait_ge(S["state_ready"], g * 4 + (c + 1))

                dve.tensor_tensor(sdm[:, :, :], repeat(cs3[:, SEQ:SEQ + 16], HPG), spread(onehot, 16), ALU.mult
                                  ).then_inc(S["sdm_ready"], 1)
                masked_decay(0)
                for h in range(2):
                    pl = c_lin(i, f"uq{h}")
                    done(pl)
                    link(dve.tensor_tensor(cols(rtmp[64:96, :]), lin_cols(pl, 96, 128), cols(ropet[96:128, :]), ALU.mult))
                    link(dve.tensor_tensor(cols(Qt[64:96, h, :]), lin_cols(pl, 64, 96), cols(ropet[64:96, :]), ALU.mult))
                    link(dve.tensor_tensor(Qt[64:96, h, :], Qt[64:96, h, :], rtmp[64:96, :], ALU.add))
                    dve.wait_ge(S["qbd_hi_s"], g * 2 + (h + 1))
                    dve.tensor_tensor(qbd_lo[64 * h:64 * h + 64, 8 * h:8 * h + 8],
                                      lin[0:64, pl.slot, 1, HALF - NB:HALF],
                                      qbd_hi[64 * h:64 * h + 64, 8 * h:8 * h + 8].bitcast(F32), ALU.subtract
                                      ).then_inc(S["lin_free"], 1)
                    dve.tensor_copy(qpe_s[64:96, :, bass.ds(g * 2 + h, 1)].rearrange("p b o -> p (b o)"),
                                    Qt[64:96, h, SEQ:T]).then_inc(S["q_ready"], 1)
                pl = c_lin(i, "uk")
                done(pl)
                dve.wait_ge(S["k_act"], g + 1)
                dve.tensor_copy(cols(Kt[0:64, 1, :]), lin_cols(pl, 64, 128)).then_inc(S["lin_free"], 1)
                pl = c_lin(i, "uv")
                done(pl)
                dve.wait_ge(S["v_act"], g + 1)
                dve.tensor_copy(V[:, 2:4, :], lin[:, pl.slot, 0, 256:512].rearrange("p (c v) -> p c v", c=2)
                                ).then_inc(S["lin_free"], 1)
                pl = c_lin(i, "ql")
                done(pl)
                for k in range(2):
                    cp = dve.tensor_copy(qlat[:, k, :, bass.ds(g * 2, 2)],
                                         lin[:, pl.slot, 0, 16 * k:16 * k + 16].rearrange("p (h b) -> p b h", h=2))
                cp.then_inc(S["lin_free"], 1)

                dve.wait_ge(S["sdec_mm"], g + 1)
                for h in range(2):
                    cp = dve.tensor_copy(sdec[64 * h:64 * h + 64, :, :],
                                         Pb[64 * h:64 * h + 64, 3, 0:64].rearrange("p (t h c) -> p t h c", t=2, h=2)
                                         [:, :, h, :])
                link(cp)
                link(dve.tensor_tensor(dtx[:, :, :], sdec[:, :, 0:8], xc[:, 0:2, SAMP0:CONVW:4], ALU.mult))
                pl = c_lin(i, "bB")
                bB = lin[:, pl.slot, :, :].rearrange("p a (b n) -> p (a b) n", b=4)
                done(pl)
                for t in range(2):
                    dve.wait_ge(S[f"st_in{t}"], g * 16 + 16)
                    link(dve.tensor_tensor(sS[:, t], sS[:, t], spread(sdec[:, t, 8:16], STATE), ALU.mult))
                    link(dve.tensor_tensor(sT[:, :, :], bB, spread(dtx[:, t, :], STATE), ALU.mult))
                    dve.tensor_tensor(sS[:, t], sS[:, t], sT[:, :, :], ALU.add).then_inc(S["st_new"], 1)
                    dve.wait_ge(S["st_new"], g * 2 + (t + 1))
                dve.nop().then_inc(S["lin_free"], 1)
                pl = c_lin(i, "bC")
                bC = lin[:, pl.slot, :, :].rearrange("p a (b n) -> p (a b) n", b=4)
                done(pl)
                for t in range(2):
                    link(dve.tensor_tensor(sT[:, :, :], bC, sS[:, t], ALU.mult))
                    link(dve.reduce_sum(ysum[:, :], sT[:, :, :], AX.X))
                    dve.scalar_tensor_tensor(yT[:, t, SEQ:T], xc[:, t, SAMP0:CONVW:4], small_of("dskip", g * 2 + t),
                                             ysum[:, :], ALU.mult, ALU.add)
                dve.nop().then_inc(S["lin_free"], 1)

                row_max(0)
                for u in range(8):
                    if u < 7:
                        row_max(u + 1)
                    normalise(u)
                    if u % 2 == 0:
                        scan_front(u // 2)
                        raw_samples(u // 2)
                    else:
                        scan_back(u // 2)
                dve.tensor_tensor(yT[:, :, :], yT[:, :, :], sz[:, :, :], ALU.mult).then_inc(S["yg_ready"], 1)
                if has_in:
                    dve.wait_ge(S["g_stat"], g + 1)
                    inverse_rms(Pb[0:TOKT, 2, 0:8], 0.25 / (D_INNER // GROUPS), S["g_diag"])
                    z_gate()
                else:
                    dve.wait_ge(S["g_stat"], g + 1)
                    inverse_rms(Pb[0:TOKT, 2, 0:8], 0.25 / (D_INNER // GROUPS), S["g_diag"])
                pl = c_lin(i, "bc")
                done(pl)
                for t in range(2):
                    dve.scalar_tensor_tensor(cols(yT[:, t, :]), cols(yT[:, t, :]), small_of("gssm", g * 2 + t),
                                             lin_cols(pl), ALU.mult, ALU.mult).then_inc(S["g_val"], 1)
                for t in range(2):
                    dve.wait_ge(S["g_hi"], g * 2 + (t + 1))
                    dve.tensor_tensor(mid_lo[:, 5 + t, :], yT[:, t, :], mid_hi[:, 5 + t, :].bitcast(F32), ALU.subtract
                                      ).then_inc(S["g_ready"], 1)
                dve.nop().then_inc(S["lin_free"], 1)
                dve.wait_ge(S["state_out"], g * 16 + 16)
                for m in range(8):
                    pl = c_lin(i, f"s{m}")
                    done(pl)
                    dve.tensor_tensor(cols(acc[:, m, :]), cols(acc[:, m, :]), lin_cols(pl), ALU.add
                                      ).then_inc(S["lin_free"], 1)
                    if has_in and m % 2:
                        conv(m // 2)
                        if m // 2:
                            silu(m // 2 - 1)
                if has_in:
                    silu(3)

            group(0)
            with dve.Fori(1, GROUPS) as i:
                chain.enter(i - 1, GROUP_LINKS)
                group(i)
            chain.leave(GROUPS - 1)
            group(GROUPS)
            dve.drain().then_inc(S["groups_over"], 1)

            for k in range(KT):
                dve.wait_ge(S["oa_hi"], k + 1)
                dve.tensor_tensor(mid_lo[:, k, 0:SEQ], o_attn[:, k, :], mid_hi[:, k, 0:SEQ].bitcast(F32), ALU.subtract
                                  ).then_inc(S["oa_ready"], 1)
            dve.wait_ge(S["groups_over"], 3)
            per = len(ROW_LIN)
            with dve.Fori(0, NB) as b:
                chain.enter(b, ROW_LINKS)

                def pl_of(name):
                    return looped(LIN_D, per, b, ROW_LIN.index(name))
                one = bass.ds(b, 1)
                dve.tensor_copy(qlb[:, :, :], qlat[:, :, one, :].rearrange("p k o h -> p k (o h)"))
                dve.tensor_copy(qpb[64:96, :], qpe_s[64:96, one, :].rearrange("p o h -> p (o h)"))
                dve.tensor_copy(snb[:, 0:2], ckv_s[:, :, one].rearrange("p k o -> p (k o)"))
                dve.tensor_copy(snb[64:96, 2:3], kpe_s[64:96, one]).then_inc(S["qb_ready"], 1)
                dve.wait_ge(S["sc_done"], b + 1)
                link(dve.reduce_max(sms[0:16, 0:1], Pb[0:16, :, :].rearrange("p a b -> p (a b)"), AX.X))
                pl = pl_of("SN")
                done(pl)
                link(dve.tensor_tensor(sms[0:16, 1:2], lin[0:16, pl.slot, 0, 0:1], sms[0:16, 0:1], ALU.max))
                dve.tensor_copy(Pexp[0:16, PAST:PAST + 1], lin[0:16, pl.slot, 0, 0:1]).then_inc(S["lin_free"], 1)
                dve.tensor_scalar(sms[0:16, 2:3], sms[0:16, 1:2], -SM_SCALE, None, ALU.mult).then_inc(S["s_bias"], 1)
                dve.wait_ge(S["s_exp"], b + 1)
                link(dve.tensor_tensor(sms[0:16, 4:5], sms[0:16, 3:4], Pexp[0:16, PAST:PAST + 1], ALU.add))
                link(dve.reciprocal(sms[0:16, 5:6], sms[0:16, 4:5]))
                dve.tensor_scalar(Pexp[0:16, 0:PAST + 1], Pexp[0:16, 0:PAST + 1], sms[0:16, 5:6], None, ALU.mult
                                  ).then_inc(S["s_prob"], 1)
                dve.wait_ge(S["s_prob"], b + 1)
                dve.tensor_scalar(pnd[:, :], ident[0:16, 0:16], Pexp[0:16, PAST:PAST + 1], None, ALU.mult
                                  ).then_inc(S["pn_ready"], 1)
                dve.wait_ge(S["ga_tanh"], b + 1)
                dve.nop().then_inc(S["lin_free"], 1)
                dve.wait_ge(S["gb_tanh"], b + 1)
                dve.scalar_tensor_tensor(at_g(acc, b), tg[:, :], 1.0, at_g(acc, b), ALU.add, ALU.mult
                                         ).then_inc(S["lin_free"], 1)
                pl = pl_of("PT")
                done(pl)
                dve.tensor_copy(PTs[:, :, :], lin[:, pl.slot, 0, 0:256].rearrange("p (j h) -> p j h", j=PAGES)
                                ).then_inc(S["lin_free"], 1)
                pl = pl_of("PN")
                done(pl)
                dve.tensor_copy(pnb[:, :], lin[:, pl.slot, 0, 0:16]).then_inc(S["lin_free"], 1)
                dve.wait_ge(S["lin_free"], pl.index + 1)
                pl = pl_of("OL")
                done(pl)
                for k in range(2):
                    ol = dve.scalar_tensor_tensor(olat[:, k, one, :].rearrange("p o h -> p (o h)"), pnb[:, :],
                                                  ckv_s[:, k, one], lin[:, pl.slot, k, 0:16], ALU.mult, ALU.add)
                ol.then_inc(S["lin_free"], 1)
            chain.leave(NB)
            dve.wait_ge(S["olat_hi_s"], 1)
            dve.tensor_tensor(olat_lo[:, :], olat[:, :, :, :].rearrange("p k b h -> p (k b h)"),
                              olat_hi[:, :].bitcast(F32), ALU.subtract).then_inc(S["olat_ready"], 1)
            for h in range(2):
                dve.wait_ge(S["ov_hi"], h + 1)
                src = lin[64 * h:64 * h + 64, LIN_OV % 2, 0, 0:128].rearrange("p (k b h) -> p k b h", k=8, h=2)
                dve.tensor_tensor(mid_lo[64 * h:64 * h + 64, :, SEQ:T], src[:, :, :, h],
                                  mid_hi[64 * h:64 * h + 64, :, SEQ:T].bitcast(F32), ALU.subtract
                                  ).then_inc(S["ov_ready"], 1)
            dve.wait_ge(S["ov_ready"], 2)
            dve.nop().then_inc(S["lin_free"], 1)
            with dve.Fori(0, KT // 2) as i:
                for j in range(2):
                    pl = looped(LIN_E, 2, i, j)
                    m = i * 2 + j
                    done(pl)
                    dve.scalar_tensor_tensor(cols(etmp[:, j, :]), cols(at_g(sga, m)), 1.0, lin_cols(pl),
                                             ALU.add, ALU.mult).then_inc(S["lin_free"], 1)
                    dve.wait_ge(S["lin_free"], pl.index + 1)
                    dve.tensor_tensor(etmp[:, j, :], etmp[:, j, :], at_g(acc, m), ALU.add).then_inc(S["mg_val"], 1)
                    dve.wait_ge(S["mg_hi"], i * 2 + (j + 1))
                    dve.tensor_tensor(at_g(act_lo, m), etmp[:, j, :], at_g(act_hi, m).bitcast(F32), ALU.subtract
                                      ).then_inc(S["mg_ready"], 1)
            dve.memset(acc[:, :, :], 0.0)
            with dve.Fori(0, KT // 2) as i:
                for j in range(2):
                    pl = looped(LIN_F, 2, i, j)
                    dve.wait_ge(S["mix_sq"], i * 2 + (j + 1))
                    dve.tensor_copy(cols(at_g(mix, i * 2 + j)), lin_cols(pl)).then_inc(S["lin_free"], 1)
            dve.wait_ge(S["n_stat"], 1)
            inverse_rms(Pb[0:TOKT, 0, 0:8], 0.25 / D_MODEL, S["n_diag"])
            dve.wait_ge(S["x_again"], 16 * 4)
            pl = fixed(LIN_N)
            done(pl)
            for k in range(KT):
                link(dve.scalar_tensor_tensor(cols(mix[:, k, :]), cols(mix[:, k, :]), small_of("gpost", k),
                                              lin_cols(pl), ALU.mult, ALU.mult))
                dve.tensor_tensor(x2[:, k, :], x2[:, k, :], mix[:, k, :], ALU.add).then_inc(S["x2_val"], 1)
            dve.nop().then_inc(S["lin_free"], 1)
            dve.wait_ge(S["n_stat"], 2)
            inverse_rms(Pb[0:TOKT, 0, 8:16], 1.0 / D_MODEL, S["n_diag"])
            normed(KT, lambda k: x2[:, k, :], lambda k: small_of("gpremlp", k), fixed(LIN_N + 1), lambda k: mix[:, k, :],
                   lambda k: act_hi[:, k, :], lambda k: act_lo[:, k, :], S["h_val"], S["h_hi"], S["h_ready"], 0)

            def up(lin_at, blk_slot, blk):
                for j in range(4):
                    pl = lin_at(j)
                    dve.wait_ge(S["relu_a"], blk * 4 + (j + 1))
                    dve.tensor_tensor(cols(relu[:, j % 2, :]), lin_cols(pl), cols(relu[:, j % 2, :]), ALU.mult
                                      ).then_inc(S["lin_free"], 1)
                    dve.wait_ge(S["f_hi"], blk * 4 + (j + 1))
                    dve.tensor_tensor(mid_lo[:, 4 * blk_slot + j, :], relu[:, j % 2, :],
                                      mid_hi[:, 4 * blk_slot + j, :].bitcast(F32), ALU.subtract
                                      ).then_inc(S["f_ready"], 1)

            def down(lin_at):
                for m in range(8):
                    pl = lin_at(m)
                    done(pl)
                    dve.tensor_tensor(cols(acc[:, m, :]), cols(acc[:, m, :]), lin_cols(pl), ALU.add
                                      ).then_inc(S["lin_free"], 1)

            up(lambda j: fixed(LIN_G + j), 0, 0)
            with dve.Fori(0, 3) as i:
                for j in range(2):
                    la = LIN_G + 4 + 12 * j
                    up(lambda k: looped(la, 24, i, k), 1 - j, i * 2 + (j + 1))
                    down(lambda k: looped(la + 4, 24, i, k))
            la = LIN_G + 76
            up(lambda k: fixed(la + k), 1, 7)
            down(lambda k: fixed(la + 4 + k))
            down(lambda k: fixed(la + 12 + k))
            dve.wait_ge(S["n_stat"], 3)
            inverse_rms(Pb[0:TOKT, 0, 0:8], 1.0 / D_MODEL, S["n_diag"])
            pl = fixed(LIN_H)
            done(pl)
            for k in range(KT):
                link(dve.scalar_tensor_tensor(cols(mix[:, k, :]), cols(acc[:, k, :]), small_of("gpostmlp", k),
                                              lin_cols(pl), ALU.mult, ALU.mult))
                dve.tensor_tensor(mix[:, k, :], mix[:, k, :], x2[:, k, :], ALU.add).then_inc(S["y_val"], 1)


INS = ["wall", "xT", "small", "ident", "amask", "smask", "ropet", "pages", "cache", "rope", "hist", "state"]
OUTS = {"yT": [P, KT, T], "kvT": [P, 2, T], "kpeT": [ROPE, T], "convT": [GROUPS, P, 4, RAWW - SEQ],
        "ssmT": [GROUPS, P, 256], "stateT": [NB, SSM_HEADS, 64, STATE]}


def tiles(w):
    return w.reshape(-1, P, w.shape[1]).transpose(1, 0, 2)


def weight_stream(w_in, w_uq, w_uk, w_uv, w_br_attn, w_br_ssm, w_out, w_up, w_down):
    b = np.cumsum([0, Q_LORA, KV_LORA, ROPE, D_INNER, CONV_DIM, SSM_HEADS, D_MODEL, D_MODEL])
    w = {n: w_in[:, b[k]:b[k + 1]] for k, n in enumerate(["q", "kv", "pe", "z", "xbc", "dt", "ga", "gb"])}
    wall = np.zeros((N_CHUNKS, P, 1024), np.float32)
    n = [0]

    def put(*parts):
        at = 0
        for x in parts:
            x = x.reshape(P, -1)
            wall[n[0], :, at:at + x.shape[1]] = x
            at += x.shape[1]
        n[0] += 1

    def cols_of(x, a):
        return tiles(x[:, a:a + P])

    pe = w["pe"]
    put(tiles(np.concatenate([w["dt"], np.zeros((D_MODEL, 32), np.float32), pe, pe[:, 16:32], pe[:, 0:16]], axis=1)))
    for k in range(3):
        put(cols_of(w["q"], k * P))
    for k in range(2):
        put(cols_of(w["kv"], k * P))

    def group_in(name, g):
        if name[0] == "x":
            put(cols_of(w["xbc"], 256 * g + P * int(name[1])))
        elif name in "bc":
            put(cols_of(w["xbc"], D_INNER + 1024 * "bc".index(name) + P * g))
        else:
            put(cols_of(w["z"], 256 * g + P * int(name[1])))

    def group_rest(name, g):
        if name == "UQ":
            u = w_uq[:, 2 * g:2 * g + 2, :]
            u = np.concatenate([u, u[:, :, 80:96], u[:, :, 64:80]], axis=2)
            put(tiles(u.reshape(Q_LORA, 256)))
        elif name == "UKV":
            uk = w_uk[:, 2 * g:2 * g + 2, :].reshape(KV_LORA, P)
            uv = w_uv[:, 2 * g:2 * g + 2, :].reshape(KV_LORA, P)
            put(tiles(uk), uk.T, tiles(uv))
        else:
            m0 = 512 * "AB".index(name[1])
            put(tiles(w_br_ssm[256 * g:256 * g + 256, m0:m0 + 512]))

    for i in range(GROUPS + 1):
        order = FIRST_CH if i == 0 else (LAST_CH if i == GROUPS else STEADY_CH)
        for name in order:
            if name in IN_LIN:
                group_in(name, i)
            else:
                group_rest(name, i - 1)
    for m in range(KT):
        put(cols_of(w["ga"], m * P))
        put(cols_of(w["gb"], m * P))
    for half in range(2):
        put(*[tiles(w_uv[:, 2 * pr:2 * pr + 2, :].reshape(KV_LORA, P)) for pr in range(4 * half, 4 * half + 4)])
    for wt in (w_br_attn, w_out):
        for m in range(KT):
            put(cols_of(wt, m * P))

    def up(blk):
        for j in range(4):
            put(cols_of(w_up, (4 * blk + j) * P))

    def down(blk):
        for m in range(4):
            put(tiles(w_down[512 * blk:512 * blk + 512, 256 * m:256 * m + 256]))

    up(0)
    for blk in range(7):
        up(blk + 1)
        down(blk)
    down(7)
    assert n[0] == N_CHUNKS, n
    return wall


def lay_out(x):
    a = {k: np.asarray(v) for k, v in x.items()}
    w = {k: a[k][0] for k in ("w_in", "w_uq", "w_uk", "w_uv", "w_br_attn", "w_br_ssm", "w_out", "w_up", "w_down")}
    out = {"wall": weight_stream(**w)}
    tok = np.concatenate([a["x_prompt"][0], a["x_sample"][:, 0]], axis=0)
    out["xT"] = tiles(tok.T)
    ch = {"x0": 0, "x1": P}
    conv = np.concatenate([a["w_conv"][0], a["b_conv"][0][None]], axis=0).T
    chan = np.array([[[256 * g + c for c in range(P)], [256 * g + P + c for c in range(P)],
                      [D_INNER + P * g + c for c in range(P)],
                      [D_INNER + 1024 + P * g + c for c in range(P)]] for g in range(GROUPS)])
    vec = {"gpre": a["g_pre_mix"][0], "gq": a["g_q"][0], "gkv": a["g_kv"][0], "gssm": a["g_ssm"][0],
           "gpost": a["g_post_mix"][0], "gpremlp": a["g_pre_mlp"][0], "gpostmlp": a["g_post_mlp"][0],
           "dskip": np.repeat(a["d_skip"][0], 64)}
    small = np.zeros((P, N_SMALL), np.float32)
    for name, (at, n) in SMALL.items():
        if name in vec:
            small[:, at:at + n] = vec[name].reshape(n, P).T
    small[0:32, SMALL["dtbias"][0]] = a["dt_bias"][0]
    small[0:32, SMALL["alog"][0]] = a["a_log"][0]
    at, n = SMALL["conv"]
    small[:, at:at + n] = conv[chan].transpose(2, 0, 1, 3).reshape(P, n)
    out["small"] = small
    i = np.arange(P)
    out["ident"] = np.eye(P, dtype=np.float32)
    out["amask"] = np.where(i[None, :] <= i[:, None], 0, NEG).astype(np.float32)
    out["smask"] = np.where(i[:, None] <= i[None, :], 0, NEG).astype(np.float32)
    half = ROPE // 2
    inv = (np.float32(10000.0) ** (-np.arange(half, dtype=np.float32) / np.float32(half))).astype(np.float32)
    pos = np.concatenate([np.arange(SEQ), np.full(NB, PAST)]).astype(np.float32)
    ang = (inv[:, None] * pos[None, :]).astype(np.float32)
    rt = np.zeros((P, T), np.float32)
    rt[64:80] = rt[80:96] = np.cos(ang)
    rt[96:112] = -np.sin(ang)
    rt[112:128] = np.sin(ang)
    out["ropet"] = rt
    out["pages"] = a["page_table"].reshape(1, -1)
    c = a["cache_kv_latent"][0]
    out["cache"] = np.concatenate([c.transpose(0, 2, 1).reshape(N_PHYS, 2, P, PAGE).transpose(0, 2, 1, 3)
                                   .reshape(N_PHYS, P, 256), c], axis=2)
    out["rope"] = a["cache_k_rope"][0].transpose(0, 2, 1)
    past = a["state_conv"][0]
    hist = np.zeros((GROUPS, P, 4, NB, 4), np.float32)
    hist[..., 0:3] = past.transpose(2, 0, 1)[chan].transpose(0, 2, 1, 3, 4)
    out["hist"] = hist.reshape(GROUPS, P, 4, 4 * NB)
    out["state"] = a["state_ssm"][0]
    return {k: np.ascontiguousarray(v) for k, v in out.items()}, chan


def give_back(r, chan):
    y = r["yT"].transpose(2, 1, 0).reshape(T, D_MODEL)
    kv = r["kvT"].transpose(2, 1, 0).reshape(T, KV_LORA)
    pe = r["kpeT"].T
    conv = np.zeros((CONV_DIM, RAWW - SEQ), np.float32)
    conv[chan.reshape(-1)] = r["convT"].transpose(0, 2, 1, 3).reshape(-1, RAWW - SEQ)
    rows = conv[:, 3:].reshape(CONV_DIM, NB, 4)[:, :, 1:4]
    ssm = r["ssmT"].reshape(GROUPS, STATE, HPG, 64).transpose(0, 2, 3, 1).reshape(SSM_HEADS, 64, STATE)
    out = (y[:SEQ][None], y[SEQ:][:, None], kv[:SEQ][None, None], pe[:SEQ][None, None], ssm[None, None],
           conv[:, 0:3].T[None, None], kv[SEQ:][None, :, None], pe[SEQ:][None, :, None], r["stateT"][None],
           rows.transpose(1, 2, 0)[None])
    return tuple(np.ascontiguousarray(x) for x in out)


def build(nc, arrays):
    d = {n: nc.dram_tensor("in_" + n, arrays[n].shape, mybir.dt.from_np(arrays[n].dtype), kind="ExternalInput").ap()
         for n in INS}
    o = {n: nc.dram_tensor("out_" + n, tuple(shape), F32, kind="ExternalOutput").ap() for n, shape in OUTS.items()}
    build_layer(nc, d, o)


def kernel(**inputs):
    import concourse.bacc as bacc
    from concourse.bass_utils import run_bass_kernel_spmd
    arrays, chan = lay_out(inputs)
    nc = bacc.Bacc("TRN2", target_bir_lowering=False, num_devices=1)
    build(nc, arrays)
    r = run_bass_kernel_spmd(nc, [{"in_" + n: arrays[n] for n in INS}], core_ids=[0])
    return give_back({n: r.results[0]["out_" + n] for n in OUTS}, chan)
```

```python
import numpy as np
import concourse.bass as bass
from concourse import mybir
from contextlib import ExitStack

F32 = mybir.dt.float32
F32R = mybir.dt.float32r
I32 = mybir.dt.int32
ALU = mybir.AluOpType
ACT = mybir.ActivationFunctionType
AX = mybir.AxisListType

P = 128
D_MODEL, SEQ, NB = 1024, 512, 8
T = SEQ + NB
HALF = T // 2
PAST, PAGE = 2048, 128
HEADS, Q_LORA, KV_LORA, NOPE, ROPE, V_DIM = 16, 384, 256, 64, 32, 64
D_INNER, SSM_HEADS, GROUPS, STATE, CONV_W = 2048, 32, 8, 128, 4
HPG = SSM_HEADS // GROUPS
CONV_DIM = D_INNER + 2 * GROUPS * STATE
D_FF = 4096
EPS = 1e-6
SM_SCALE = 1.0 / float(np.sqrt(NOPE + ROPE))
NEG = -1e30
CHUNK = 128
NCH = SEQ // CHUNK
KT = D_MODEL // P
TOKT = 65
N_PHYS = 160
PAGES = PAST // PAGE
RAWW = 3 + SEQ + 4 * NB
CONVW = RAWW - 3
SAMP0 = SEQ + 3

IN_LIN = ["x0", "x1", "b", "c", "z0", "z1"]
HEAD_LIN = ["uq0", "uq1", "uk", "uv", "ql", "bB"]
TAIL_LIN = ["bc"] + [f"s{m}" for m in range(8)]
FIRST_LIN = IN_LIN
STEADY_LIN = HEAD_LIN + ["x0", "sA0", "x1", "bC", "sA1", "b", "sA2", "c", "sA3", "z0", "z1"] + TAIL_LIN
LAST_LIN = HEAD_LIN + ["sA0", "bC", "sA1", "sA2", "sA3"] + TAIL_LIN
FIRST_CH = IN_LIN
STEADY_CH = ["UQ", "UKV"] + IN_LIN + ["SA", "SB"]
LAST_CH = ["UQ", "UKV", "SA", "SB"]
PRE_LIN = ["bcx", "misc", "q0", "q1", "q2", "kv0", "kv1", "bcq", "bckv"]
PRE_CH = ["misc", "q0", "q1", "q2", "kv0", "kv1"]

ROW_LIN = ["SN", "ga", "gb", "PT", "OL", "OT"]
LIN_C = len(PRE_LIN)
LIN_D = LIN_C + len(FIRST_LIN) + 7 * len(STEADY_LIN) + len(LAST_LIN)
LIN_OV = LIN_D + NB * len(ROW_LIN)
LIN_E = LIN_OV + 1
LIN_F = LIN_E + KT
LIN_N = LIN_F + KT
LIN_G = LIN_N + 2
LIN_H = LIN_G + 8 * 12
CH_C = len(PRE_CH)
CH_D = CH_C + len(FIRST_CH) + 7 * len(STEADY_CH) + len(LAST_CH)
CH_OV = CH_D + 2 * NB
CH_E = CH_OV + 2
CH_F = CH_E + KT
CH_G = CH_F + KT
N_CHUNKS = CH_G + 8 * 8


GROUP_LINKS = 67
ROW_LINKS = 10


class Place:

    def __init__(self, index, slot, turn):
        self.index, self.slot, self.turn = index, slot, turn

    def next(self):
        return Place(self.index + 1, 1 - self.slot, self.turn + self.slot)


def fixed(n):
    return Place(n, n % 2, n // 2)


def looped(base, per, i, k):
    return Place(i * per + (base + k), (base + k) % 2, i * (per // 2) + (base + k) // 2)


def c_place(base, first, steady, last, i, name):
    if isinstance(i, int) and i == 0:
        return fixed(base + first.index(name))
    start = base + len(first)
    if isinstance(i, int) and i == GROUPS:
        return fixed(start + 7 * len(steady) + last.index(name))
    return looped(start, len(steady), i - 1, steady.index(name))


def c_lin(i, name):
    return c_place(LIN_C, FIRST_LIN, STEADY_LIN, LAST_LIN, i, name)


def c_chunk(i, name):
    return c_place(CH_C, FIRST_CH, STEADY_CH, LAST_CH, i, name)


class Chain:

    def __init__(self, eng, sem):
        self.eng, self.sem, self.base, self.local, self.i, self.per = eng, sem, 0, 0, 0, 0

    def link(self, ins):
        self.local += 1
        ins.then_inc(self.sem, 1)
        self.eng.wait_ge(self.sem, self.i * self.per + (self.base + self.local))

    def enter(self, i, per):
        self.base += self.local
        self.local, self.i, self.per = 0, i, per

    def leave(self, trips):
        assert self.local == self.per, f"links per iteration: {self.local}, stated {self.per}"
        self.base += trips * self.per
        self.local, self.i, self.per = 0, 0, 0


SMALL = {}
ARENA = 16708
SEMAPHORES = """w_loaded0 w_loaded1 w_split w_used w_hi_done dve_chain act_chain lin_done lin_free
    x_in consts_in ones_set pe_gate sp_gate act_gate exp_alog sq_x stat_done rstd_diag norm_val norm_hi act_ready
    dt_raw kpe_ready lat_sq sp_ln cs_ready rows_tr rows_ready kv_val kv_out kpe_out arena_free
    hist_in conv_out raw_act conv_acc conv_tanh xc_ready qbd_hi_s q_ready k_act v_act
    sdm_ready sdec_mm st_in0 st_in1 st_new st_out0 st_out1 scores max_bias exp_done prob_ready
    pt_done pt_ready pv_done o_ready csm_ready a_row a_seg a_exp b_ready y_done state_ready state_out
    yg_ready sqg_ready g_stat g_diag g_val g_hi g_ready z_tanh groups_over
    oa_hi oa_ready pg_k0 pg_k1 pg_r qb_ready sc_done s_bias s_exp  pn_ready ga_tanh gb_tanh
    olat_hi_s olat_ready ov_hi ov_ready mg_val mg_hi mg_ready
    x_sum mix_sum x2_sum acc_sum mix_sq x_again n_stat n_diag x2_val x2_sq h_val h_hi h_ready relu_a f_hi f_ready acc_sq y_val y_out""".split()


def _lay_small():
    at = 0
    for name, n in (("gpre", 8), ("gq", 3), ("gkv", 2), ("gssm", 16), ("gpost", 8), ("gpremlp", 8),
                    ("gpostmlp", 8), ("dskip", 16), ("dtbias", 1), ("alog", 1), ("conv", 8 * 4 * 5)):
        SMALL[name] = (at, n)
        at += n
    return at


N_SMALL = _lay_small()


def build_layer(nc, d, o):
    ctx = ExitStack()
    with ctx:
        def sb(name, shape, dt=F32):
            return ctx.enter_context(nc.sbuf_tensor(name, shape, dt))

        def sem(name):
            return ctx.enter_context(nc.semaphore(name))

        w_stage = sb("w_stage", [P, 2, 1024])
        w_hi = sb("w_hi", [P, 2, 1024], F32R)
        w_lo = sb("w_lo", [P, 2, 1024], F32R)
        act_hi = sb("act_hi", [P, KT, T], F32R)
        act_lo = sb("act_lo", [P, KT, T], F32R)
        mid_hi = sb("mid_hi", [P, KT, T], F32R)
        mid_lo = sb("mid_lo", [P, KT, T], F32R)
        acc = sb("acc", [P, KT, T])
        o_attn = sb("o_attn", [P, KT, SEQ])
        qbd_hi = sb("qbd_hi", [P, 16], F32R)
        qbd_lo = sb("qbd_lo", [P, 16], F32R)
        olat_hi = sb("olat_hi", [P, 256], F32R)
        olat_lo = sb("olat_lo", [P, 256], F32R)
        small = sb("small", [P, N_SMALL])
        ident = sb("ident", [P, P])
        amask = sb("amask", [P, P])
        smask = sb("smask", [P, P])
        ropet = sb("ropet", [P, T])
        ones = sb("ones", [P, P])
        rows = sb("rows", [P, 2, NCH, SSM_HEADS])
        cs3 = sb("cs3", [SSM_HEADS, SEQ + 16])
        csm = sb("csm", [SSM_HEADS, HPG, CHUNK])
        sdm = sb("sdm", [SSM_HEADS, HPG, 16])
        sdec = sb("sdec", [P, 2, 16])
        dtx = sb("dtx", [P, 2, NB])
        ysum = sb("ysum", [P, NB])
        qlat = sb("qlat", [P, 2, NB, HEADS])
        qpe_s = sb("qpe_s", [P, NB, HEADS])
        kpe_s = sb("kpe_s", [P, NB])
        ckv_s = sb("ckv_s", [P, 2, NB])
        qlb = sb("qlb", [P, 2, HEADS])
        qpb = sb("qpb", [P, HEADS])
        olat = sb("olat", [P, 2, NB, HEADS])
        pages = sb("pages", [1, NB * PAGES], I32)
        st = sb("st", [P, 3, 8])
        diag_flat = sb("diag", [P, T])
        diag = diag_flat[:, :].rearrange("p (c t) -> p c t", c=8)
        snb = sb("snb", [P, 3])
        sm = sb("sm", [P, 8])
        sms = sb("sms", [P, 8])
        pnd = sb("pnd", [16, 16])
        pnb = sb("pnb", [P, 16])
        ahead = sb("ahead", [SSM_HEADS, 1])

        arena = sb("arena", [P, ARENA])
        at = [0]

        def part(n, pat=None, **kw):
            v = arena[:, at[0]:at[0] + n]
            at[0] += n
            assert at[0] <= ARENA, at[0]
            return v.rearrange(pat, **kw) if pat else v

        x_sb = part(KT * T, "p (k t) -> p k t", k=KT)
        sq = part(KT * T, "p (k t) -> p k t", k=KT)
        lat = part(5 * T, "p (k t) -> p k t", k=5)
        dtw = part(5 * T, "p (k t) -> p k t", k=5)
        at[0] = 0
        raw = part(4 * RAWW, "p (k t) -> p k t", k=4)
        Kt = part(2 * T, "p (h t) -> p h t", h=2)
        xc = part(4 * CONVW, "p (k t) -> p k t", k=4)
        cacc_flat = part(2 * CONVW)
        cacc = cacc_flat.rearrange("p (k t) -> p k t", k=2)
        sC = cacc_flat[:, 0:NB * STATE].rearrange("p (b n) -> p b n", b=NB)
        sz = part(2 * T, "p (k t) -> p k t", k=2)
        yT = part(2 * T, "p (k t) -> p k t", k=2)
        state = part(256)
        sT = arena[:, at[0]:at[0] + 1024].rearrange("p (b n) -> p b n", b=NB)
        sqg = arena[:, at[0]:at[0] + 2 * T].rearrange("p (k t) -> p k t", k=2)
        seg = part(512, "p (h l) -> p h l", h=HPG)
        ecs = part(512, "p (h l) -> p h l", h=HPG)
        rtmp = arena[:, at[0]:at[0] + T]
        Mt = part(512, "p (h l) -> p h l", h=HPG)
        Cx = part(512, "p (h l) -> p h l", h=HPG)
        xdt = part(256)
        xdte = part(256)
        Brow = part(128)
        V = part(512, "p (c v) -> p c v", c=NCH)
        Pq = part(1024, "p (u s) -> p u s", u=2)
        PT = part(512)
        sS = part(2048, "p (t b n) -> p t b n", t=2, b=NB)
        Qt = part(2 * T, "p (h t) -> p h t", h=2)
        at[0] = 0
        kT0 = part(PAGES * 256, "p (j c) -> p j c", j=PAGES)
        kT1 = o_attn[:, :, :].rearrange("p k t -> p (k t)").rearrange("p (j c) -> p j c", j=PAGES)
        kr = part(PAGES * 256, "p (j c) -> p j c", j=PAGES)
        ropek = part(PAGES * PAGE, "p (j t) -> p j t", j=PAGES)
        Pexp = part(PAST + 4)
        PTs = part(256, "p (j h) -> p j h", j=PAGES)
        sga = part(KT * T, "p (k t) -> p k t", k=KT)
        tg = diag_flat
        ol_sb = diag_flat[0:16, 0:256]
        at[0] = 0
        x2 = part(KT * T, "p (k t) -> p k t", k=KT)
        etmp = arena[:, at[0]:at[0] + 2 * T].rearrange("p (k t) -> p k t", k=2)
        mix = part(KT * T, "p (k t) -> p k t", k=KT)
        sq2 = part(KT * T, "p (k t) -> p k t", k=KT)
        relu = part(2 * T + 68)[:, 68:].rearrange("p (k t) -> p k t", k=2)
        sqsum = part(T, "p (k t) -> p k t", k=1)

        lin = ctx.enter_context(nc.psum_tensor("lin", [P, 2, 2, 512], F32))
        Pb = ctx.enter_context(nc.psum_tensor("Pb", [P, 4, 512], F32))

        def small_of(name, k=0):
            a, _ = SMALL[name]
            return small[:, bass.ds(k + a, 1)] if not isinstance(k, int) else small[:, a + k:a + k + 1]

        def lin_cols(pl, lo=0, hi=P):
            return lin[lo:hi, pl.slot, :, 0:HALF]

        def cols(ap2d):
            return ap2d.rearrange("p (a b) -> p a b", a=2)

        def at_g(ap3, g):
            if isinstance(g, int):
                return ap3[:, g, :]
            return ap3[:, bass.ds(g, 1), :].rearrange("p a b -> p (a b)")

        def spread(ap2, n):
            p_, a_ = ap2.shape
            return ap2.rearrange("p (a o) -> p a o", o=1).to_broadcast([p_, a_, n])

        def repeat(ap2, n):
            p_, a_ = ap2.shape
            return ap2.rearrange("p (o a) -> p o a", o=1).to_broadcast([p_, n, a_])

        S = {n: sem(n) for n in SEMAPHORES}
        block = ctx.enter_context(nc.Block())

        @block.sync
        def _(sp):
            def load_chunk(n, slot):
                sp.dma_start(w_stage[:, slot, :],
                             d["wall"][bass.ds(n, 1), :, :].rearrange("a p c -> p (a c)") if not isinstance(n, int)
                             else d["wall"][n, :, :]).then_inc(S[f"w_loaded{slot}"], 16)

            def next_chunk(n, slot):
                sp.wait_ge(S["w_split"], n - 1)
                load_chunk(n, slot)

            def stream(first, last):
                pairs = (last - first) // 2
                with sp.Fori(0, pairs) as i:
                    for j in range(2):
                        next_chunk(i * 2 + (first + j), (first + j) % 2)
                if (last - first) % 2:
                    next_chunk(last - 1, (last - 1) % 2)

            for k in range(4):
                sp.dma_start(x_sb[:, 2 * k:2 * k + 2, :], d["xT"][:, 2 * k:2 * k + 2, :]).then_inc(S["x_in"], 16)
            for dst, name in ((small, "small"), (ident, "ident"), (ropet, "ropet"), (amask, "amask"),
                              (smask, "smask"), (pages, "pages")):
                sp.dma_start(dst[:, :], d[name]).then_inc(S["consts_in"], 16)
            load_chunk(0, 0)
            load_chunk(1, 1)
            stream(2, CH_D + 2)

            sp.wait_ge(S["groups_over"], 3)
            for n in ("st_out0", "st_out1", "state_out", "conv_out"):
                sp.wait_ge(S[n], 16 * GROUPS)
            sp.wait_ge(S["kpe_out"], 16)

            def load_keys(b, odd):
                lo = 64 + 32 * odd
                for j in range(PAGES):
                    page = sp.value_load(pages[0:1, bass.ds(b * PAGES + j, 1)], min_val=0, max_val=N_PHYS - 1)
                    sp.dma_start((kT0, kT1)[odd][:, j, :],
                                 d["cache"][bass.ds(page, 1), :, 0:256].rearrange("a p c -> p (a c)")
                                 ).then_inc(S[f"pg_k{odd}"], 16)
                    sp.dma_start(ropek[lo:lo + 32, j, :],
                                 d["rope"][bass.ds(page, 1), :, :].rearrange("a p c -> p (a c)")
                                 ).then_inc(S[f"pg_k{odd}"], 16)

            load_keys(0, 0)
            sp.wait_ge(S["oa_ready"], KT)
            load_keys(1, 1)
            for j in range(2):
                next_chunk(CH_D + 2 + j, (CH_D + j) % 2)
            with sp.Fori(1, NB // 2) as i:
                for odd in range(2):
                    sp.wait_ge(S["sc_done"], i * 2 + (odd - 1))
                    sp.sem_inc(S["sp_gate"], 1)
                    load_keys(i * 2 + odd, odd)
                    for j in range(2):
                        next_chunk(i * 4 + (CH_D + 2 * odd + j), (CH_D + j) % 2)
            stream(CH_OV, CH_F)
            sp.wait_ge(S["lin_free"], LIN_OV)
            for k in range(4):
                sp.dma_start(x2[:, 2 * k:2 * k + 2, :], d["xT"][:, 2 * k:2 * k + 2, :]).then_inc(S["x_again"], 16)
            stream(CH_F, N_CHUNKS)
            for k in range(KT):
                sp.wait_ge(S["y_val"], k + 1)
                sp.dma_start(o["yT"][:, k, :], mix[:, k, :]).then_inc(S["y_out"], 16)
            sp.wait_ge(S["y_out"], 16 * KT)

        @block.gpsimd
        def _(pool):
            def split(first, last):
                with pool.Fori(0, (last - first) // 2) as i:
                    for j in range(2):
                        slot = (first + j) % 2
                        pool.wait_ge(S["w_hi_done"], i * 2 + (first + j + 1))
                        pool.tensor_tensor(w_lo[:, slot, :], w_stage[:, slot, :], w_hi[:, slot, :].bitcast(F32),
                                           ALU.subtract).then_inc(S["w_split"], 1)

            split(0, CH_G)
            pool.wait_ge(S["n_stat"], 1)
            for k in range(KT):
                pool.wait_ge(S["x2_sq"], k + 1)
                if k == 0:
                    pool.tensor_copy(sqsum[:, 0, :], sq2[:, 0, :]).then_inc(S["x2_sum"], 1)
                else:
                    pool.wait_ge(S["x2_sum"], k)
                    pool.tensor_tensor(sqsum[:, 0, :], sqsum[:, 0, :], sq2[:, k, :], ALU.add).then_inc(S["x2_sum"], 1)
            split(CH_G, N_CHUNKS)

        @block.tensor
        def _(pe):
            def free_slot(pl):
                if not isinstance(pl.index, int) or pl.index >= 2:
                    pe.wait_ge(S["lin_free"], pl.index - 1)

            def open_chunk(ch, first_matmul):
                if not isinstance(ch.index, int) or ch.index >= 1:
                    first_matmul.then_inc(S["w_used"], 1)

            def linear(pl, ch, offs, rhs, opens=True, between=None, rhs_ready=None):
                if opens:
                    pe.wait_ge(S["w_split"], ch.index + 1)
                free_slot(pl)
                n = len(offs)
                first = True
                for k, (off, (rh, rl)) in enumerate(zip(offs, rhs)):
                    if between and k == 3 * n // 4:
                        between()
                    if rhs_ready:
                        pe.wait_ge(rhs_ready, k + 1)
                    for w, r, p in ((w_hi, rh, 0), (w_hi, rl, 1), (w_lo, rh, 2)):
                        for hf in range(2):
                            mm = pe.matmul(lin[:, pl.slot, hf, 0:HALF], w[:, ch.slot, off:off + P],
                                           r[:, hf * HALF:(hf + 1) * HALF],
                                           start=(k == 0 and p == 0), stop=(k == n - 1 and p == 2))
                            if first and opens:
                                open_chunk(ch, mm)
                            first = False
                mm.then_inc(S["lin_done"], 1)

            def act_rhs(n=KT):
                return [(act_hi[:, k, :], act_lo[:, k, :]) for k in range(n)]

            def mid_rhs(a, n):
                return [(mid_hi[:, k, :], mid_lo[:, k, :]) for k in range(a, a + n)]

            def statistics(out, src, n):
                for c in range(8):
                    for k in range(n):
                        mm = pe.matmul(out[:, c:c + 1], src[:, k, TOKT * c:TOKT * (c + 1)], ones[:, 0:1],
                                       start=(k == 0), stop=(k == n - 1))
                return mm

            def broadcast_stat(pl):
                free_slot(pl)
                for hf in range(2):
                    mm = pe.matmul(lin[:, pl.slot, hf, 0:HALF], ones[0:TOKT, :], diag[0:TOKT, 4 * hf:4 * hf + 4, :],
                                   start=True, stop=True)
                mm.then_inc(S["lin_done"], 1)

            K8 = [k * P for k in range(KT)]
            pe.wait_ge(S["ones_set"], 1)
            pe.wait_ge(S["consts_in"], 16 * 6)
            pe.wait_ge(S["x_sum"], 1)
            statistics(Pb[0:TOKT, 2, 0:8], sq, 2).then_inc(S["stat_done"], 1)
            pe.wait_ge(S["rstd_diag"], 1)
            broadcast_stat(fixed(0))
            for k in range(6):
                linear(fixed(1 + k), fixed(k), K8, act_rhs(), rhs_ready=S["act_ready"] if k == 0 else None)
            pe.wait_ge(S["lat_sq"], 3)
            statistics(Pb[0:TOKT, 2, 8:16], sq[:, 0:3, :], 3).then_inc(S["stat_done"], 1)
            pe.wait_ge(S["lat_sq"], 5)
            statistics(Pb[0:TOKT, 0, 0:8], sq[:, 3:5, :], 2).then_inc(S["stat_done"], 1)
            pe.wait_ge(S["rstd_diag"], 2)
            broadcast_stat(fixed(7))
            pe.wait_ge(S["rstd_diag"], 3)
            broadcast_stat(fixed(8))
            pe.wait_ge(S["cs_ready"], 1)
            for c in range(NCH):
                pe.transpose(Pb[:, 3, 32 * c:32 * c + 32], cs3[:, CHUNK * c:CHUNK * (c + 1)], ident[0:32, 0:32])
            for c in range(NCH):
                tr = pe.transpose(Pb[:, 3, 128 + 32 * c:160 + 32 * c], dtw[0:32, 0, CHUNK * c:CHUNK * (c + 1)],
                                  ident[0:32, 0:32])
            tr.then_inc(S["rows_tr"], 1)

            def group(i):
                has_in = not (isinstance(i, int) and i == GROUPS)
                has_rest = not (isinstance(i, int) and i == 0)
                g = i - 1

                def project(name, between=None):
                    if has_in:
                        linear(c_lin(i, name), c_chunk(i, name), K8, act_rhs(), between=between)

                if not has_rest:
                    for name in IN_LIN:
                        project(name)
                    return

                def scores(u):
                    h, q, pb = u // 4, u % 4, u % 2
                    if u >= 2:
                        pe.wait_ge(S["o_ready"], g * 8 + (u - 1))
                    pe.matmul(Pb[:, pb, 0:(q + 1) * P], Qt[0:96, h, q * P:(q + 1) * P], Kt[0:96, h, 0:(q + 1) * P],
                              start=True, stop=False)
                    pe.matmul(Pb[:, pb, q * P:(q + 1) * P], ident[:, :], amask[:, :],
                              start=False, stop=True).then_inc(S["scores"], 1)

                def transposes(u):
                    q, pb = u % 4, u % 2
                    pe.wait_ge(S["prob_ready"], g * 8 + (u + 1))
                    for j in range(q + 1):
                        tr = pe.transpose(Pb[:, 2, j * P:(j + 1) * P], Pq[:, pb, j * P:(j + 1) * P], ident[:, :])
                    tr.then_inc(S["pt_done"], 1)

                def values(u):
                    h, q, pb = u // 4, u % 4, u % 2
                    pe.wait_ge(S["pt_ready"], g * 8 + (u + 1))
                    for j in range(q + 1):
                        mm = pe.matmul(Pb[64 * h:64 * h + 64, pb, 0:P], V[:, j, 64 * h:64 * h + 64],
                                       PT[:, j * P:(j + 1) * P], start=(j == 0), stop=(j == q))
                    mm.then_inc(S["pv_done"], 1)

                def scan_front(c):
                    pl = c_lin(i, f"sA{c}")
                    free_slot(pl)
                    pe.wait_ge(S["csm_ready"], g * 4 + (c + 1))
                    tok = slice(CHUNK * c, CHUNK * (c + 1))
                    pe.matmul(lin[:, pl.slot, 0, :], ones[0:32, :], csm[:, :, :], start=True, stop=True)
                    for t in range(3):
                        pe.transpose(lin[:, pl.slot, 1, t * P:(t + 1) * P], xc[:, t, tok], ident[:, :])
                    pe.matmul(lin[:, pl.slot, 1, 3 * P:4 * P], xc[:, 2, tok], xc[:, 3, tok],
                              start=True, stop=True).then_inc(S["lin_done"], 1)

                def scan_back(c):
                    pe.wait_ge(S["b_ready"], g * 4 + (c + 1))
                    if c:
                        pe.wait_ge(S["state_ready"], g * 4 + c)
                    for h in range(HPG):
                        out = Pb[64 * (h % 2):64 * (h % 2) + 64, 3, P * (h // 2):P * (h // 2) + P]
                        pe.matmul(out, xdt[:, 64 * h:64 * h + 64], Mt[:, h, :], start=True, stop=(c == 0))
                        if c:
                            pe.matmul(out, state[:, 64 * h:64 * h + 64], Cx[:, h, :], start=False, stop=True)
                    pe.matmul(Pb[:, 3, 256:512], Brow[:, :], xdte[:, :], start=True, stop=True
                              ).then_inc(S["y_done"], 1)

                pe.wait_ge(S["act_ready"], KT + 5)
                for h in range(2):
                    linear(c_lin(i, f"uq{h}"), c_chunk(i, "UQ"), [k * 256 + h * P for k in range(3)], mid_rhs(0, 3),
                           opens=(h == 0))
                ch = c_chunk(i, "UKV")
                linear(c_lin(i, "uk"), ch, [0, P], mid_rhs(3, 2))
                pl = c_lin(i, "uv")
                free_slot(pl)
                for c in range(NCH):
                    for k in range(2):
                        tok = slice(CHUNK * c, CHUNK * (c + 1))
                        a, b = mid_hi[:, 3 + k, tok], mid_lo[:, 3 + k, tok]
                        wh = w_hi[:, ch.slot, 512 + k * P:640 + k * P]
                        wl = w_lo[:, ch.slot, 512 + k * P:640 + k * P]
                        for n, (x, w) in enumerate(((a, wh), (a, wl), (b, wh))):
                            mm = pe.matmul(lin[:, pl.slot, 0, c * P:(c + 1) * P], x, w,
                                           start=(k == 0 and n == 0), stop=(k == 1 and n == 2))
                mm.then_inc(S["lin_done"], 1)
                pl = c_lin(i, "ql")
                free_slot(pl)
                pe.wait_ge(S["lin_free"], c_lin(i, "uq1").index + 1)
                for k in range(2):
                    out = lin[:, pl.slot, 0, 16 * k:16 * k + 16]
                    for n, (w, r) in enumerate(((w_hi, qbd_hi), (w_hi, qbd_lo), (w_lo, qbd_hi))):
                        mm = pe.matmul(out, w[:, ch.slot, 256 + k * P:384 + k * P], r[:, :],
                                       start=(n == 0), stop=(n == 2))
                mm.then_inc(S["lin_done"], 1)
                pe.wait_ge(S["sdm_ready"], g + 1)
                pe.matmul(Pb[:, 3, 0:64], ones[0:32, :], sdm[:, :, :], start=True, stop=True
                          ).then_inc(S["sdec_mm"], 1)
                pe.wait_ge(S["xc_ready"], g * 4 + 4)

                def on_all(name, k):
                    pl = c_lin(i, name)
                    free_slot(pl)
                    for b in range(NB):
                        mm = pe.matmul(lin[:, pl.slot, b // 4, (b % 4) * P:(b % 4 + 1) * P],
                                       xc[:, k, SAMP0 + 4 * b:SAMP0 + 4 * b + 1].to_broadcast([P, P]), ident[:, :],
                                       start=True, stop=True)
                    mm.then_inc(S["lin_done"], 1)

                on_all("bB", 2)
                pe.wait_ge(S["q_ready"], g * 2 + 2)
                pe.wait_ge(S["lin_free"], c_lin(i, "uv").index + 1)
                scores(0)
                project("x0")
                for c in range(NCH):
                    u = 2 * c
                    scan_front(c)
                    scores(u + 1)
                    if has_in:
                        project(IN_LIN[c + 1], between=lambda: transposes(u))
                    else:
                        transposes(u)
                    if c == 0:
                        on_all("bC", 3)
                    values(u)
                    if has_in and c == NCH - 1:
                        project("z1", between=lambda: transposes(u + 1))
                    else:
                        transposes(u + 1)
                    scan_back(c)
                    if c < NCH - 1:
                        scores(u + 2)
                    values(u + 1)
                pe.wait_ge(S["o_ready"], g * 8 + 8)
                pe.wait_ge(S["sqg_ready"], g + 1)
                statistics(Pb[0:TOKT, 2, 0:8], sqg, 2).then_inc(S["g_stat"], 1)
                pe.wait_ge(S["g_diag"], g + 1)
                broadcast_stat(c_lin(i, "bc"))
                pe.wait_ge(S["g_ready"], g * 2 + 2)
                for m in range(8):
                    linear(c_lin(i, f"s{m}"), c_chunk(i, "SA" if m < 4 else "SB"),
                           [(m % 4) * P, 512 + (m % 4) * P], mid_rhs(5, 2), opens=(m % 4 == 0))

            group(0)
            with pe.Fori(1, GROUPS) as i:
                group(i)
            group(GROUPS)
            pe.drain().then_inc(S["groups_over"], 1)

            per = len(ROW_LIN)

            def row(i, odd):
                b = i * 2 + odd
                lo = 64 + 32 * odd

                def pl_of(name):
                    return looped(LIN_D, 2 * per, i, odd * per + ROW_LIN.index(name))
                pe.wait_ge(S["qb_ready"], b + 1)
                pl = pl_of("SN")
                free_slot(pl)
                for k in range(2):
                    pe.matmul(lin[0:16, pl.slot, 0, 0:1], qlb[:, k, :], snb[:, k:k + 1], start=(k == 0), stop=False)
                pe.matmul(lin[0:16, pl.slot, 0, 0:1], qpb[lo:lo + 32, :], snb[lo:lo + 32, 2:3], start=False, stop=True
                          ).then_inc(S["lin_done"], 1)
                pe.wait_ge(S[f"pg_k{odd}"], i * (32 * PAGES) + 32 * PAGES)
                for n in range(4):
                    for k in range(2):
                        pe.matmul(Pb[0:16, n, :], qlb[:, k, :], (kT0, kT1)[odd][:, 4 * n:4 * n + 4, k * P:(k + 1) * P],
                                  start=(k == 0), stop=False)
                    mm = pe.matmul(Pb[0:16, n, :], qpb[lo:lo + 32, :], ropek[lo:lo + 32, 4 * n:4 * n + 4, :],
                                   start=False, stop=True)
                mm.then_inc(S["sc_done"], 1)
                for j, name in enumerate(("ga", "gb")):
                    linear(pl_of(name), looped(CH_D, 4, i, 2 * odd + j), K8, act_rhs())
                pl = pl_of("PT")
                free_slot(pl)
                pe.wait_ge(S["s_exp"], b + 1)
                pe.sem_inc(S["pe_gate"], 1)
                for j in range(PAGES):
                    tr = pe.transpose(lin[:, pl.slot, 0, 16 * j:16 * j + 16], Pexp[0:16, j * P:(j + 1) * P],
                                      ident[0:16, 0:16])
                tr.then_inc(S["lin_done"], 1)
                pl = pl_of("OL")
                free_slot(pl)
                pe.wait_ge(S["lin_free"], pl_of("PT").index + 1)
                pe.wait_ge(S["pg_r"], b * (16 * PAGES) + 16 * PAGES)
                for j in range(PAGES):
                    mm = pe.matmul(lin[0:16, pl.slot, 0, 0:256], PTs[:, j, :], kr[:, j, :],
                                   start=(j == 0), stop=(j == PAGES - 1))
                mm.then_inc(S["lin_done"], 1)
                pl = pl_of("OT")
                free_slot(pl)
                pe.wait_ge(S["pn_ready"], b + 1)
                pe.matmul(lin[:, pl.slot, 1, 0:16], ones[0:16, :], pnd[:, :], start=True, stop=True)
                pe.wait_ge(S["lin_free"], pl_of("OL").index + 1)
                pe.sem_inc(S["pe_gate"], 1)
                for k in range(2):
                    tr = pe.transpose(lin[:, pl.slot, 0, 16 * k:16 * k + 16], ol_sb[:, k * P:(k + 1) * P],
                                      ident[0:16, 0:16])
                tr.then_inc(S["lin_done"], 1)

            with pe.Fori(0, NB // 2) as i:
                for odd in range(2):
                    row(i, odd)

            pl = fixed(LIN_OV)
            free_slot(pl)
            pe.wait_ge(S["olat_ready"], 1)
            for pr in range(8):
                ch = fixed(CH_OV + pr // 4)
                if pr % 4 == 0:
                    pe.wait_ge(S["w_split"], ch.index + 1)
                for k in range(2):
                    off = (pr % 4) * 256 + k * P
                    view = [x[:, k * P:(k + 1) * P].rearrange("p (b h) -> p b h", b=NB)[:, :, 2 * pr:2 * pr + 2]
                            for x in (olat_hi, olat_lo)]
                    for n, (w, r) in enumerate(((w_hi, view[0]), (w_hi, view[1]), (w_lo, view[0]))):
                        mm = pe.matmul(lin[:, pl.slot, 0, 16 * pr:16 * pr + 16], w[:, ch.slot, off:off + P], r,
                                       start=(k == 0 and n == 0), stop=(k == 1 and n == 2))
                        if pr % 4 == 0 and k == 0 and n == 0:
                            open_chunk(ch, mm)
            mm.then_inc(S["lin_done"], 1)

            pe.wait_ge(S["oa_ready"], KT)
            pe.wait_ge(S["ov_ready"], 2)
            with pe.Fori(0, KT // 2) as i:
                for j in range(2):
                    linear(looped(LIN_E, 2, i, j), looped(CH_E, 2, i, j), K8, mid_rhs(0, KT))
            pe.wait_ge(S["mg_ready"], KT)
            with pe.Fori(0, KT // 2) as i:
                for j in range(2):
                    linear(looped(LIN_F, 2, i, j), looped(CH_F, 2, i, j), K8, act_rhs())
            pe.wait_ge(S["mix_sum"], KT)
            statistics(Pb[0:TOKT, 0, 0:8], sqsum, 1).then_inc(S["n_stat"], 1)
            pe.wait_ge(S["n_diag"], 1)
            broadcast_stat(fixed(LIN_N))
            pe.wait_ge(S["x2_sum"], KT)
            statistics(Pb[0:TOKT, 0, 8:16], sqsum, 1).then_inc(S["n_stat"], 1)
            pe.wait_ge(S["n_diag"], 2)
            broadcast_stat(fixed(LIN_N + 1))
            def up(lin_at, ch_at, first=False):
                for j in range(4):
                    linear(lin_at(j), ch_at(j), K8, act_rhs(), rhs_ready=S["h_ready"] if first and j == 0 else None)

            def down(lin_at, ch_at, blk_slot, blk):
                pe.wait_ge(S["f_ready"], blk * 4 + 4)
                for m in range(8):
                    linear(lin_at(m), ch_at(m // 2), [k * 256 + (m % 2) * P for k in range(4)],
                           mid_rhs(4 * blk_slot, 4), opens=(m % 2 == 0))

            up(lambda j: fixed(LIN_G + j), lambda j: fixed(CH_G + j), first=True)
            with pe.Fori(0, 3) as i:
                for j in range(2):
                    la, ca = LIN_G + 4 + 12 * j, CH_G + 4 + 8 * j
                    up(lambda k: looped(la, 24, i, k), lambda k: looped(ca, 16, i, k))
                    down(lambda k: looped(la + 4, 24, i, k), lambda k: looped(ca + 4, 16, i, k), j, i * 2 + j)
            la, ca = LIN_G + 4 + 72, CH_G + 4 + 48
            up(lambda k: fixed(la + k), lambda k: fixed(ca + k))
            down(lambda k: fixed(la + 4 + k), lambda k: fixed(ca + 4 + k), 0, 6)
            down(lambda k: fixed(la + 12 + k), lambda k: fixed(ca + 8 + k), 1, 7)
            pe.wait_ge(S["acc_sum"], KT)
            statistics(Pb[0:TOKT, 0, 0:8], sqsum, 1).then_inc(S["n_stat"], 1)
            pe.wait_ge(S["n_diag"], 3)
            broadcast_stat(fixed(LIN_H))

        @block.scalar
        def _(act):
            chain = Chain(act, S["act_chain"])

            def done(pl):
                act.wait_ge(S["lin_done"], pl.index + 1)

            def round_chunk(ch):
                act.wait_ge(S[f"w_loaded{ch.slot}"], ch.turn * 16 + 16)
                if not (isinstance(ch.index, int) and ch.index < 2):
                    act.wait_ge(S["w_used"], ch.index - 1)
                act.activation(w_hi[:, ch.slot, :], w_stage[:, ch.slot, :], ACT.Copy).then_inc(S["w_hi_done"], 1)

            for k in range(4):
                act.wait_ge(S["x_in"], 16 * 4)
                act.activation(sq[:, 2 * k:2 * k + 2, :], x_sb[:, 2 * k:2 * k + 2, :], ACT.Square
                               ).then_inc(S["sq_x"], 1)
            act.wait_ge(S["consts_in"], 16 * 6)
            act.activation(ahead[:, :], small_of("alog")[0:32, :], ACT.Exp).then_inc(S["exp_alog"], 1)
            round_chunk(fixed(0))
            for k in range(KT):
                act.wait_ge(S["norm_val"], k + 1)
                act.activation(act_hi[:, k, :], sq[:, k, :], ACT.Copy).then_inc(S["norm_hi"], 1)
            round_chunk(fixed(1))
            done(fixed(1))
            act.activation(cols(dtw[0:32, 0, :]), lin_cols(fixed(1), 0, 32), ACT.Identity,
                           bias=small_of("dtbias")[0:32, :]).then_inc(S["dt_raw"], 1)
            for k in range(5):
                round_chunk(fixed(2 + k))
                done(fixed(2 + k))
                act.activation(cols(sq[:, k, :]), lin_cols(fixed(2 + k)), ACT.Square).then_inc(S["lat_sq"], 1)
            chain.link(act.activation(dtw[0:32, 1, :], dtw[0:32, 0, :], ACT.Abs))
            chain.link(act.activation(dtw[0:32, 1, :], dtw[0:32, 1, :], ACT.Exp, scale=-1.0))
            act.activation(dtw[0:32, 3, :], dtw[0:32, 1, :], ACT.Ln, bias=1.0).then_inc(S["sp_ln"], 1)
            for k in range(5):
                act.wait_ge(S["norm_val"], KT + k + 1)
                act.activation(mid_hi[:, k, :], sq[:, k, :], ACT.Copy).then_inc(S["norm_hi"], 1)
            act.dma_start(o["kvT"], sq[:, 3:5, :]).then_inc(S["kv_out"], 16)
            act.dma_start(o["kpeT"], Kt[64:96, 0, :]).then_inc(S["kpe_out"], 16)
            act.wait_ge(S["cs_ready"], 1)
            act.activation(cs3[:, SEQ + 8:SEQ + 16], dtw[0:32, 0, SEQ:T], ACT.Exp, scale=ahead[:, :]
                           ).then_inc(S["sp_ln"], 1)
            act.wait_ge(S["kv_out"], 16)
            act.wait_ge(S["rows_ready"], 1)

            def group(i):
                has_in = not (isinstance(i, int) and i == GROUPS)
                has_rest = not (isinstance(i, int) and i == 0)
                g = i - 1
                hist = d["hist"]
                def history():
                    if has_rest:
                        act.wait_ge(S["xc_ready"], i * 4)
                        act.wait_ge(S["conv_out"], i * 16)
                        act.dma_start(raw[:, :, SAMP0:RAWW],
                                      hist[bass.ds(i, 1)].rearrange("a p k c -> p (a k) c")).then_inc(S["hist_in"], 16)
                    else:
                        act.dma_start(raw[:, :, SAMP0:RAWW], hist[0]).then_inc(S["hist_in"], 16)

                def raw_evac(k, between=None):
                    if has_in:
                        round_chunk(c_chunk(i, IN_LIN[k]).next())
                    if between:
                        between()
                    if has_in:
                        pl = c_lin(i, IN_LIN[k])
                        done(pl)
                        act.activation(raw[:, k, 3:3 + HALF], lin[:, pl.slot, 0, 0:HALF], ACT.Copy)
                        act.activation(raw[:, k, 3 + HALF:3 + SEQ], lin[:, pl.slot, 1, 0:SEQ - HALF], ACT.Copy
                                       ).then_inc(S["raw_act"], 1)

                def z_evac():
                    for k in range(2):
                        pl = c_lin(i, f"z{k}")
                        if not has_rest:
                            round_chunk(c_chunk(i, f"z{k}").next())
                        done(pl)
                        act.activation(cols(sz[:, k, :]), lin_cols(pl), ACT.Tanh, scale=0.5
                                       ).then_inc(S["z_tanh"], 1)

                def conv_tanh(k):
                    act.wait_ge(S["conv_acc"], i * 4 + (k + 1))
                    act.activation(xc[:, k, :], cacc[:, k % 2, :], ACT.Tanh).then_inc(S["conv_tanh"], 1)

                def finish_inputs():
                    if has_rest:
                        conv_tanh(2)
                        round_chunk(c_chunk(i, "SB").next())
                        conv_tanh(3)
                    act.wait_ge(S["lin_free"], c_lin(i, "c").index + 1)
                    act.dma_start(o["convT"][bass.ds(i, 1)].rearrange("a p k c -> p (a k) c") if has_rest
                                  else o["convT"][0], raw[:, :, SEQ:RAWW]).then_inc(S["conv_out"], 16)
                    for t in range(2):
                        if has_rest:
                            act.wait_ge(S[f"st_out{t}"], i * 16)
                        src = d["state"][:, bass.ds(i * 4 + 2 * t, 2), :, :] if has_rest \
                            else d["state"][:, 2 * t:2 * t + 2, :, :]
                        act.dma_start(sS[:, t], src.rearrange("b h p n -> (h p) b n")).then_inc(S[f"st_in{t}"], 16)

                if not has_rest:
                    history()
                    for k in range(4):
                        raw_evac(k)
                        if k:
                            conv_tanh(k - 1)
                    z_evac()
                    conv_tanh(3)
                    finish_inputs()
                    return

                def exponent(u):
                    q, pb = u % 4, u % 2
                    act.wait_ge(S["max_bias"], g * 8 + (u + 1))
                    act.activation(Pq[:, pb, 0:(q + 1) * P], Pb[:, pb, 0:(q + 1) * P], ACT.Exp,
                                   bias=sm[:, 2 + pb:3 + pb], scale=SM_SCALE, accum_out=sm[:, 4 + pb:5 + pb]
                                   ).then_inc(S["exp_done"], 1)

                round_chunk(c_chunk(i, "UKV"))
                for h in range(2):
                    pl = c_lin(i, f"uq{h}")
                    done(pl)
                    act.activation(cols(Qt[0:64, h, :]), lin_cols(pl, 0, 64), ACT.Copy)
                    act.activation(qbd_hi[64 * h:64 * h + 64, 8 * h:8 * h + 8], lin[0:64, pl.slot, 1, HALF - NB:HALF],
                                   ACT.Copy).then_inc(S["qbd_hi_s"], 1)
                pl = c_lin(i, "uk")
                round_chunk(c_chunk(i, "UKV").next())
                done(pl)
                act.activation(cols(Kt[0:64, 0, :]), lin_cols(pl, 0, 64), ACT.Copy).then_inc(S["k_act"], 1)
                pl = c_lin(i, "uv")
                done(pl)
                act.activation(V[:, 0:2, :], lin[:, pl.slot, 0, 0:256].rearrange("p (c v) -> p c v", c=2), ACT.Copy
                               ).then_inc(S["v_act"], 1)
                if has_in:
                    history()
                raw_evac(0)
                exponent(0)
                def weights_out(u):
                    q = u % 4
                    act.wait_ge(S["pt_done"], g * 8 + (u + 1))
                    act.activation(PT[:, 0:(q + 1) * P], Pb[:, 2, 0:(q + 1) * P], ACT.Copy).then_inc(S["pt_ready"], 1)

                def output_out(u):
                    h, q, pb = u // 4, u % 4, u % 2
                    act.wait_ge(S["pv_done"], g * 8 + (u + 1))
                    act.activation(at_g(o_attn[64 * h:64 * h + 64], g)[:, q * P:(q + 1) * P],
                                   Pb[64 * h:64 * h + 64, pb, 0:P], ACT.Copy).then_inc(S["o_ready"], 1)

                for c in range(NCH):
                    u = 2 * c
                    pl = c_lin(i, f"sA{c}")
                    done(pl)
                    if c:
                        act.wait_ge(S["state_ready"], g * 4 + c)
                    act.activation(Brow[:, :], lin[:, pl.slot, 1, 256:384], ACT.Copy).then_inc(S["a_row"], 1)
                    exponent(u + 1)
                    act.wait_ge(S["a_seg"], g * 4 + (c + 1))
                    act.activation(ecs[:, :, :], lin[:, pl.slot, 0, :].rearrange("p (h l) -> p h l", h=HPG),
                                   ACT.Exp)
                    act.activation(seg[:, :, :], seg[:, :, :], ACT.Exp).then_inc(S["a_exp"], 1)
                    if c < NCH - 1:
                        raw_evac(c + 1, between=lambda: weights_out(u))
                    else:
                        if has_in:
                            round_chunk(c_chunk(i, "z1"))
                        weights_out(u)
                    output_out(u)
                    if has_in and c == NCH - 1:
                        round_chunk(c_chunk(i, "z1").next())
                    weights_out(u + 1)
                    if c < NCH - 1:
                        exponent(u + 2)
                    output_out(u + 1)
                    if c == 0:
                        for t in range(2):
                            act.wait_ge(S["st_new"], g * 2 + (t + 1))
                            act.dma_start(o["stateT"][:, bass.ds(g * 4 + 2 * t, 2), :, :].rearrange(
                                "b h p n -> (h p) b n"), sS[:, t]).then_inc(S[f"st_out{t}"], 16)
                act.wait_ge(S["state_ready"], g * 4 + 4)
                act.dma_start(o["ssmT"][bass.ds(g, 1)].rearrange("a p c -> p (a c)"), state[:, :]
                              ).then_inc(S["state_out"], 16)
                act.wait_ge(S["yg_ready"], g + 1)
                act.activation(sqg[:, :, :], yT[:, :, :], ACT.Square).then_inc(S["sqg_ready"], 1)
                if has_in:
                    z_evac()
                    conv_tanh(0)
                    conv_tanh(1)
                for t in range(2):
                    act.wait_ge(S["g_val"], g * 2 + (t + 1))
                    act.activation(mid_hi[:, 5 + t, :], yT[:, t, :], ACT.Copy).then_inc(S["g_hi"], 1)
                round_chunk(c_chunk(i, "SB"))
                if has_in:
                    finish_inputs()
                else:
                    round_chunk(c_chunk(i, "SB").next())

            group(0)
            with act.Fori(1, GROUPS) as i:
                group(i)
            group(GROUPS)
            act.drain().then_inc(S["groups_over"], 1)

            def load_rows(b, first, last):
                for j in range(first, last):
                    page = act.value_load(pages[0:1, bass.ds(b * PAGES + j, 1)], min_val=0, max_val=N_PHYS - 1)
                    act.dma_start(kr[:, j, :], d["cache"][bass.ds(page, 1), :, 256:512].rearrange("a p c -> p (a c)")
                                  ).then_inc(S["pg_r"], 16)

            for k in range(KT):
                act.wait_ge(S["lin_done"], LIN_D)
                act.activation(mid_hi[:, k, 0:SEQ], o_attn[:, k, :], ACT.Copy).then_inc(S["oa_hi"], 1)
            act.wait_ge(S["groups_over"], 3)
            for n in ("st_out0", "st_out1", "state_out", "conv_out"):
                act.wait_ge(S[n], 16 * GROUPS)
            act.wait_ge(S["kpe_out"], 16)
            load_rows(0, 0, 10)
            round_chunk(fixed(CH_D + 1))
            per = len(ROW_LIN)

            def row(b, last):
                def pl_of(name):
                    return looped(LIN_D, per, b, ROW_LIN.index(name))
                act.wait_ge(S["s_bias"], b + 1)
                act.activation(Pexp[0:16, 0:PAST], Pb[0:16, :, :].rearrange("p a b -> p (a b)"), ACT.Exp,
                               bias=sms[0:16, 2:3], scale=SM_SCALE, accum_out=sms[0:16, 3:4])
                act.activation(Pexp[0:16, PAST:PAST + 1], Pexp[0:16, PAST:PAST + 1], ACT.Exp,
                               bias=sms[0:16, 2:3], scale=SM_SCALE).then_inc(S["s_exp"], 1)
                load_rows(b, 10, PAGES)
                done(pl_of("ga"))
                act.activation(cols(at_g(sga, b)), lin_cols(pl_of("ga")), ACT.Tanh, scale=0.5
                               ).then_inc(S["ga_tanh"], 1)
                done(pl_of("gb"))
                act.activation(cols(tg[:, :]), lin_cols(pl_of("gb")), ACT.Tanh, scale=0.5).then_inc(S["gb_tanh"], 1)
                round_chunk(looped(CH_D, 2, b, 2))
                if not last:
                    act.wait_ge(S["lin_done"], pl_of("OL").index + 1)
                    act.sem_inc(S["act_gate"], 1)
                    load_rows(b + 1, 0, 10)
                    round_chunk(looped(CH_D, 2, b, 3))

            with act.Fori(0, NB - 1) as b:
                row(b, False)
            row(NB - 1, True)
            act.wait_ge(S["lin_free"], LIN_OV)
            act.activation(olat_hi[:, :], olat[:, :, :, :].rearrange("p k b h -> p (k b h)"), ACT.Copy
                           ).then_inc(S["olat_hi_s"], 1)
            round_chunk(fixed(CH_OV + 1))
            round_chunk(fixed(CH_E))
            done(fixed(LIN_OV))
            for h in range(2):
                src = lin[64 * h:64 * h + 64, LIN_OV % 2, 0, 0:128].rearrange("p (k b h) -> p k b h", k=8, h=2)
                act.activation(mid_hi[64 * h:64 * h + 64, :, SEQ:T], src[:, :, :, h], ACT.Copy).then_inc(S["ov_hi"], 1)
            with act.Fori(0, KT // 2) as i:
                for j in range(2):
                    round_chunk(looped(CH_E, 2, i, j + 1))
                    act.wait_ge(S["mg_val"], i * 2 + (j + 1))
                    act.activation(at_g(act_hi, i * 2 + j), etmp[:, j, :], ACT.Copy).then_inc(S["mg_hi"], 1)
            with act.Fori(0, KT // 2) as i:
                for j in range(2):
                    pl = looped(LIN_F, 2, i, j)
                    round_chunk(looped(CH_F, 2, i, j + 1))
                    done(pl)
                    act.activation(cols(at_g(sq2, i * 2 + j)), lin_cols(pl), ACT.Square).then_inc(S["mix_sq"], 1)
            for k in range(KT):
                act.wait_ge(S["x2_val"], k + 1)
                act.activation(sq2[:, k, :], x2[:, k, :], ACT.Square).then_inc(S["x2_sq"], 1)
            for k in range(KT):
                act.wait_ge(S["h_val"], k + 1)
                act.activation(act_hi[:, k, :], mix[:, k, :], ACT.Copy).then_inc(S["h_hi"], 1)

            def up(lin_at, ch_at, blk_slot):
                for j in range(4):
                    pl = lin_at(j)
                    round_chunk(ch_at(j + 1))
                    done(pl)
                    act.activation(cols(relu[:, j % 2, :]), lin_cols(pl), ACT.Relu).then_inc(S["relu_a"], 1)
                    act.wait_ge(S["lin_free"], pl.index + 1)
                    act.activation(mid_hi[:, 4 * blk_slot + j, :], relu[:, j % 2, :], ACT.Copy
                                   ).then_inc(S["f_hi"], 1)

            def down(ch_at):
                for j in range(4):
                    round_chunk(ch_at(j + 1))

            up(lambda j: fixed(LIN_G + j), lambda j: fixed(CH_G + j), 0)
            with act.Fori(0, 3) as i:
                for j in range(2):
                    la, ca = LIN_G + 4 + 12 * j, CH_G + 4 + 8 * j
                    up(lambda k: looped(la, 24, i, k), lambda k: looped(ca, 16, i, k), 1 - j)
                    down(lambda k: looped(ca + 4, 16, i, k))
            ca = CH_G + 4 + 48
            up(lambda k: fixed(LIN_G + 76 + k), lambda k: fixed(ca + k), 1)
            down(lambda k: fixed(ca + 4 + k))
            for k in range(KT):
                if k % 2 == 0 and k < 6:
                    round_chunk(fixed(ca + 9 + k // 2))
                act.wait_ge(S["lin_free"], LIN_H - KT + k + 1)
                act.activation(sq2[:, k, :], acc[:, k, :], ACT.Square).then_inc(S["acc_sq"], 1)

        @block.vector
        def _(dve):
            chain = Chain(dve, S["dve_chain"])
            link = chain.link

            def done(pl):
                dve.wait_ge(S["lin_done"], pl.index + 1)

            def inverse_rms(src, mean_scale, signal):
                ms, y, t = st[0:TOKT, 0, :], st[0:TOKT, 1, :], st[0:TOKT, 2, :]
                link(dve.tensor_scalar(ms, src, mean_scale, EPS, ALU.mult, ALU.add))
                link(dve.tensor_single_scalar(y.bitcast(I32), ms.bitcast(I32), 1, ALU.logical_shift_right))
                link(dve.tensor_scalar(y.bitcast(I32), y.bitcast(I32), -1.0, float(0x5f3759df), ALU.mult, ALU.add))
                for _ in range(3):
                    link(dve.tensor_tensor(t, y, y, ALU.mult))
                    link(dve.scalar_tensor_tensor(t, t, -0.5, ms, ALU.mult, ALU.mult))
                    link(dve.scalar_tensor_tensor(y, t, 1.5, y, ALU.add, ALU.mult))
                dve.tensor_tensor(diag[0:TOKT], repeat(ident[0:TOKT, 0:TOKT], 8), spread(y, TOKT), ALU.mult
                                  ).then_inc(signal, 1)

            def normed(n, src, gain, pl, val, hi_of, lo_of, s_val, s_hi, s_ready, base):
                done(pl)

                def low(k):
                    dve.wait_ge(s_hi, base + k + 1)
                    dve.tensor_tensor(lo_of(k), val(k), hi_of(k).bitcast(F32), ALU.subtract).then_inc(s_ready, 1)
                for k in range(n):
                    dve.scalar_tensor_tensor(cols(val(k)), cols(src(k)), gain(k), lin_cols(pl), ALU.mult, ALU.mult
                                             ).then_inc(s_val, 1)
                    if k:
                        low(k - 1)
                low(n - 1)
                dve.nop().then_inc(S["lin_free"], 1)

            dve.memset(ones[:, :], 1.0).then_inc(S["ones_set"], 1)
            dve.memset(qbd_hi[:, :].bitcast(F32), 0.0)
            dve.memset(qbd_lo[:, :].bitcast(F32), 0.0)
            dve.memset(acc[:, :, :], 0.0)
            dve.wait_ge(S["consts_in"], 16 * 6)
            for name in ("conv", "gssm", "gpost"):
                a, n = SMALL[name]
                link(dve.tensor_scalar(small[:, a:a + n], small[:, a:a + n], 0.5, None, ALU.mult))
            dve.wait_ge(S["exp_alog"], 1)
            link(dve.tensor_scalar(ahead[:, :], ahead[:, :], -1.0, None, ALU.mult))
            for k in range(1, 4):
                dve.wait_ge(S["sq_x"], k + 1)
                add = dve.tensor_tensor(sq[:, 0:2, :], sq[:, 0:2, :], sq[:, 2 * k:2 * k + 2, :], ALU.add)
                if k < 3:
                    link(add)
            add.then_inc(S["x_sum"], 1)
            dve.wait_ge(S["stat_done"], 1)
            inverse_rms(Pb[0:TOKT, 2, 0:8], 1.0 / D_MODEL, S["rstd_diag"])
            normed(KT, lambda k: x_sb[:, k, :], lambda k: small_of("gpre", k), fixed(0), lambda k: sq[:, k, :],
                   lambda k: act_hi[:, k, :], lambda k: act_lo[:, k, :],
                   S["norm_val"], S["norm_hi"], S["act_ready"], 0)
            done(fixed(1))
            link(dve.tensor_tensor(cols(x_sb[64:96, 7, :]), lin_cols(fixed(1), 96, 128), cols(ropet[96:128, :]), ALU.mult))
            link(dve.tensor_tensor(cols(Kt[64:96, 0, :]), lin_cols(fixed(1), 64, 96), cols(ropet[64:96, :]), ALU.mult))
            link(dve.tensor_tensor(Kt[64:96, 0, :], Kt[64:96, 0, :], x_sb[64:96, 7, :], ALU.add))
            dve.tensor_copy(Kt[64:96, 1, :], Kt[64:96, 0, :])
            dve.wait_ge(S["dt_raw"], 1)
            dve.tensor_copy(kpe_s[64:96, :], Kt[64:96, 0, SEQ:T]).then_inc(S["lin_free"], 1)
            for k in range(5):
                done(fixed(2 + k))
                dve.wait_ge(S["lat_sq"], k + 1)
                dve.tensor_copy(cols(lat[:, k, :]), lin_cols(fixed(2 + k))).then_inc(S["lin_free"], 1)
            dve.wait_ge(S["stat_done"], 2)
            inverse_rms(Pb[0:TOKT, 2, 8:16], 1.0 / Q_LORA, S["rstd_diag"])
            normed(3, lambda k: lat[:, k, :], lambda k: small_of("gq", k), fixed(7), lambda k: sq[:, k, :],
                   lambda k: mid_hi[:, k, :], lambda k: mid_lo[:, k, :],
                   S["norm_val"], S["norm_hi"], S["act_ready"], KT)
            dve.wait_ge(S["stat_done"], 3)
            inverse_rms(Pb[0:TOKT, 0, 0:8], 1.0 / KV_LORA, S["rstd_diag"])
            normed(2, lambda k: lat[:, 3 + k, :], lambda k: small_of("gkv", k), fixed(8), lambda k: sq[:, 3 + k, :],
                   lambda k: mid_hi[:, 3 + k, :], lambda k: mid_lo[:, 3 + k, :],
                   S["norm_val"], S["norm_hi"], S["act_ready"], KT + 3)
            dve.tensor_copy(ckv_s[:, :, :], sq[:, 3:5, SEQ:T])
            dve.wait_ge(S["sp_ln"], 1)
            x_, e_, u_, l_, m_ = [dtw[0:32, k, :] for k in range(5)]
            link(dve.tensor_scalar(u_, e_, 1.0, -1.0, ALU.add, ALU.add))
            link(dve.tensor_scalar(m_, u_, 0.0, None, ALU.is_equal))
            link(dve.tensor_tensor(u_, u_, m_, ALU.add))
            link(dve.tensor_tensor(l_, l_, m_, ALU.add))
            link(dve.reciprocal(u_, u_))
            link(dve.tensor_tensor(l_, l_, u_, ALU.mult))
            link(dve.tensor_tensor(l_, l_, e_, ALU.mult))
            link(dve.scalar_tensor_tensor(x_, x_, 0.0, l_, ALU.max, ALU.add))
            link(dve.tensor_scalar(u_[:, 0:SEQ], x_[:, 0:SEQ], ahead[:, :], None, ALU.mult))
            dve.memset(m_[:, 0:CHUNK], 1.0)
            link(dve.tensor_copy(cs3[:, SEQ:SEQ + NB], x_[:, SEQ:T]))
            for c in range(NCH):
                last = dve.tensor_tensor_scan(cs3[:, CHUNK * c:CHUNK * (c + 1)], m_[:, 0:CHUNK],
                                              u_[:, CHUNK * c:CHUNK * (c + 1)], 0.0, ALU.mult, ALU.add)
            last.then_inc(S["cs_ready"], 1)
            dve.wait_ge(S["rows_tr"], 1)
            dve.tensor_copy(rows[:, :, :, :].rearrange("p a c h -> p (a c h)"), Pb[:, 3, 0:256]
                            ).then_inc(S["rows_ready"], 1)
            dve.wait_ge(S["sp_ln"], 2)
            dve.wait_ge(S["rows_ready"], 1)
            dve.wait_ge(S["norm_hi"], KT + 5)
            link(dve.memset(raw[:, :, 0:3], 0.0))

            def group(i):
                has_in = not (isinstance(i, int) and i == GROUPS)
                has_rest = not (isinstance(i, int) and i == 0)
                g = i - 1

                def raw_samples(k):
                    if has_in:
                        pl = c_lin(i, IN_LIN[k])
                        done(pl)
                        if k == 0:
                            dve.wait_ge(S["hist_in"], i * 16 + 16)
                        dve.wait_ge(S["raw_act"], i * 4 + (k + 1))
                        dve.tensor_copy(raw[:, k, SAMP0 + 3:RAWW:4], lin[:, pl.slot, 1, HALF - NB:HALF]
                                        ).then_inc(S["lin_free"], 1)

                def z_gate():
                    for k in range(2):
                        dve.wait_ge(S["z_tanh"], i * 2 + (k + 1))
                        pl = c_lin(i, f"z{k}")
                        dve.scalar_tensor_tensor(cols(sz[:, k, :]), cols(sz[:, k, :]), 1.0, lin_cols(pl),
                                                 ALU.add, ALU.mult).then_inc(S["lin_free"], 1)

                def conv(k, half=None):
                    def tap(n):
                        return small_of("conv", i * 20 + (5 * k + n))
                    a = cacc[:, k % 2, :]
                    if half != 1:
                        dve.wait_ge(S["lin_free"], c_lin(i, IN_LIN[k]).index + 1)
                        if k >= 2:
                            dve.wait_ge(S["xc_ready"], i * 4 + (k - 1))
                        elif has_rest:
                            dve.wait_ge(S["xc_ready"], i * 4)
                        link(dve.tensor_scalar(a, raw[:, k, 0:CONVW], tap(0), tap(4), ALU.mult, ALU.add))
                        link(dve.scalar_tensor_tensor(a, raw[:, k, 1:1 + CONVW], tap(1), a, ALU.mult, ALU.add))
                    if half != 0:
                        link(dve.scalar_tensor_tensor(a, raw[:, k, 2:2 + CONVW], tap(2), a, ALU.mult, ALU.add))
                        dve.scalar_tensor_tensor(a, raw[:, k, 3:3 + CONVW], tap(3), a, ALU.mult, ALU.add
                                                 ).then_inc(S["conv_acc"], 1)

                def silu(k):
                    dve.wait_ge(S["conv_tanh"], i * 4 + (k + 1))
                    dve.scalar_tensor_tensor(xc[:, k, :], xc[:, k, :], 1.0, cacc[:, k % 2, :], ALU.add, ALU.mult
                                             ).then_inc(S["xc_ready"], 1)

                if not has_rest:
                    for k in range(4):
                        raw_samples(k)
                        if k:
                            silu(k - 1)
                        conv(k)
                    z_gate()
                    silu(3)
                    return

                onehot = ident[0:32, bass.ds(g * 4, 4)]

                def masked_decay(c):
                    dve.tensor_tensor(csm[:, :, :], repeat(cs3[:, CHUNK * c:CHUNK * (c + 1)], HPG),
                                      spread(onehot, CHUNK), ALU.mult).then_inc(S["csm_ready"], 1)

                def row_max(u):
                    q, pb = u % 4, u % 2
                    dve.wait_ge(S["scores"], g * 8 + (u + 1))
                    link(dve.reduce_max(sm[:, pb:pb + 1], Pb[:, pb, 0:(q + 1) * P], AX.X))
                    dve.tensor_scalar(sm[:, 2 + pb:3 + pb], sm[:, pb:pb + 1], -SM_SCALE, None, ALU.mult
                                      ).then_inc(S["max_bias"], 1)

                def normalise(u):
                    q, pb = u % 4, u % 2
                    dve.wait_ge(S["exp_done"], g * 8 + (u + 1))
                    link(dve.reciprocal(sm[:, 6 + pb:7 + pb], sm[:, 4 + pb:5 + pb]))
                    dve.tensor_scalar(Pq[:, pb, 0:(q + 1) * P], Pq[:, pb, 0:(q + 1) * P], sm[:, 6 + pb:7 + pb],
                                      None, ALU.mult).then_inc(S["prob_ready"], 1)

                def scan_front(c):
                    pl = c_lin(i, f"sA{c}")
                    done(pl)
                    tok = slice(CHUNK * c, CHUNK * (c + 1))
                    heads = bass.ds(g * 4, 4)
                    link(dve.tensor_tensor(seg[:, :, :], lin[:, pl.slot, 0, :].rearrange("p (h l) -> p h l", h=HPG),
                                           spread(rows[:, 0, c, heads], CHUNK), ALU.subtract))
                    dve.tensor_tensor(seg[:, :, :], seg[:, :, :], repeat(smask[:, :], HPG), ALU.min
                                      ).then_inc(S["a_seg"], 1)
                    dve.wait_ge(S["a_row"], g * 4 + (c + 1))
                    link(dve.tensor_tensor(xdt[:, :].rearrange("p (h d) -> p h d", h=HPG),
                                           lin[:, pl.slot, 1, 0:256].rearrange("p (h d) -> p h d", h=HPG),
                                           spread(rows[:, 1, c, heads], 64), ALU.mult))
                    dve.wait_ge(S["a_exp"], g * 4 + (c + 1))
                    dve.tensor_tensor(xdte[:, :].rearrange("p (h d) -> p h d", h=HPG),
                                      xdt[:, :].rearrange("p (h d) -> p h d", h=HPG),
                                      seg[:, :, CHUNK - 1:CHUNK].to_broadcast([P, HPG, 64]), ALU.mult)
                    dve.tensor_tensor(Mt[:, :, :], repeat(lin[:, pl.slot, 1, 384:512], HPG), seg[:, :, :], ALU.mult
                                      ).then_inc(S["lin_free"], 1)
                    dve.tensor_tensor(Cx[:, :, :], ecs[:, :, :], repeat(xc[:, 3, tok], HPG), ALU.mult
                                      ).then_inc(S["b_ready"], 1)
                    if c < NCH - 1:
                        masked_decay(c + 1)

                def scan_back(c):
                    dve.wait_ge(S["y_done"], g * 4 + (c + 1))
                    for t in range(2):
                        y = dve.scalar_tensor_tensor(yT[:, t, CHUNK * c:CHUNK * (c + 1)],
                                                     xc[:, t, CHUNK * c:CHUNK * (c + 1)], small_of("dskip", g * 2 + t),
                                                     Pb[:, 3, P * t:P * (t + 1)], ALU.mult, ALU.add)
                    if c == 0:
                        dve.tensor_copy(state[:, :], Pb[:, 3, 256:512]).then_inc(S["state_ready"], 1)
                        dve.wait_ge(S["state_ready"], g * 4 + 1)
                        return
                    link(dve.tensor_tensor(state[:, :].rearrange("p (h d) -> p h d", h=HPG),
                                           state[:, :].rearrange("p (h d) -> p h d", h=HPG),
                                           ecs[:, :, CHUNK - 1:CHUNK].to_broadcast([P, HPG, 64]), ALU.mult))
                    dve.tensor_tensor(state[:, :], state[:, :], Pb[:, 3, 256:512], ALU.add
                                      ).then_inc(S["state_ready"], 1)
                    dve.wait_ge(S["state_ready"], g * 4 + (c + 1))

                dve.tensor_tensor(sdm[:, :, :], repeat(cs3[:, SEQ:SEQ + 16], HPG), spread(onehot, 16), ALU.mult
                                  ).then_inc(S["sdm_ready"], 1)
                masked_decay(0)
                for h in range(2):
                    pl = c_lin(i, f"uq{h}")
                    done(pl)
                    link(dve.tensor_tensor(cols(rtmp[64:96, :]), lin_cols(pl, 96, 128), cols(ropet[96:128, :]), ALU.mult))
                    link(dve.tensor_tensor(cols(Qt[64:96, h, :]), lin_cols(pl, 64, 96), cols(ropet[64:96, :]), ALU.mult))
                    link(dve.tensor_tensor(Qt[64:96, h, :], Qt[64:96, h, :], rtmp[64:96, :], ALU.add))
                    dve.wait_ge(S["qbd_hi_s"], g * 2 + (h + 1))
                    dve.tensor_tensor(qbd_lo[64 * h:64 * h + 64, 8 * h:8 * h + 8],
                                      lin[0:64, pl.slot, 1, HALF - NB:HALF],
                                      qbd_hi[64 * h:64 * h + 64, 8 * h:8 * h + 8].bitcast(F32), ALU.subtract
                                      ).then_inc(S["lin_free"], 1)
                    dve.tensor_copy(qpe_s[64:96, :, bass.ds(g * 2 + h, 1)].rearrange("p b o -> p (b o)"),
                                    Qt[64:96, h, SEQ:T]).then_inc(S["q_ready"], 1)
                pl = c_lin(i, "uk")
                done(pl)
                dve.wait_ge(S["k_act"], g + 1)
                dve.tensor_copy(cols(Kt[0:64, 1, :]), lin_cols(pl, 64, 128)).then_inc(S["lin_free"], 1)
                pl = c_lin(i, "uv")
                done(pl)
                dve.wait_ge(S["v_act"], g + 1)
                dve.tensor_copy(V[:, 2:4, :], lin[:, pl.slot, 0, 256:512].rearrange("p (c v) -> p c v", c=2)
                                ).then_inc(S["lin_free"], 1)
                pl = c_lin(i, "ql")
                done(pl)
                for k in range(2):
                    cp = dve.tensor_copy(qlat[:, k, :, bass.ds(g * 2, 2)],
                                         lin[:, pl.slot, 0, 16 * k:16 * k + 16].rearrange("p (h b) -> p b h", h=2))
                cp.then_inc(S["lin_free"], 1)

                dve.wait_ge(S["sdec_mm"], g + 1)
                for h in range(2):
                    cp = dve.tensor_copy(sdec[64 * h:64 * h + 64, :, :],
                                         Pb[64 * h:64 * h + 64, 3, 0:64].rearrange("p (t h c) -> p t h c", t=2, h=2)
                                         [:, :, h, :])
                link(cp)
                link(dve.tensor_tensor(dtx[:, :, :], sdec[:, :, 0:8], xc[:, 0:2, SAMP0:CONVW:4], ALU.mult))
                for t in range(2):
                    dve.wait_ge(S[f"st_in{t}"], g * 16 + 16)
                    link(dve.tensor_tensor(sS[:, t], sS[:, t], spread(sdec[:, t, 8:16], STATE), ALU.mult))
                pl = c_lin(i, "bB")
                bB = lin[:, pl.slot, :, :].rearrange("p a (b n) -> p (a b) n", b=4)
                done(pl)
                for t in range(2):
                    link(dve.tensor_tensor(sT[:, :, :], bB, spread(dtx[:, t, :], STATE), ALU.mult))
                    dve.tensor_tensor(sS[:, t], sS[:, t], sT[:, :, :], ALU.add).then_inc(S["st_new"], 1)
                    dve.wait_ge(S["st_new"], g * 2 + (t + 1))
                dve.nop().then_inc(S["lin_free"], 1)
                raw_samples(0)
                row_max(0)

                def sample_y(t):
                    pl = c_lin(i, "bC")
                    if t == 0:
                        dve.wait_ge(S["xc_ready"], i * 4)
                        done(pl)
                    bC = lin[:, pl.slot, :, :].rearrange("p a (b n) -> p (a b) n", b=4)
                    link(dve.tensor_tensor(sC[:, :, :], bC, sS[:, t], ALU.mult))
                    if t == 1:
                        dve.nop().then_inc(S["lin_free"], 1)
                    link(dve.reduce_sum(ysum[:, :], sC[:, :, :], AX.X))
                    dve.scalar_tensor_tensor(yT[:, t, SEQ:T], xc[:, t, SAMP0:CONVW:4], small_of("dskip", g * 2 + t),
                                             ysum[:, :], ALU.mult, ALU.add)

                for c in range(NCH):
                    u = 2 * c
                    normalise(u)
                    row_max(u + 1)
                    scan_front(c)
                    if c < NCH - 1:
                        raw_samples(c + 1)
                    normalise(u + 1)
                    if c == 0:
                        sample_y(0)
                    if has_in and c in (1, 2):
                        conv(c - 1, 0)
                    scan_back(c)
                    if c < NCH - 1:
                        row_max(u + 2)
                    if c == 0:
                        sample_y(1)
                    if has_in and c in (1, 2):
                        conv(c - 1, 1)
                dve.tensor_tensor(yT[:, :, :], yT[:, :, :], sz[:, :, :], ALU.mult).then_inc(S["yg_ready"], 1)
                if has_in:
                    dve.wait_ge(S["g_stat"], g + 1)
                    inverse_rms(Pb[0:TOKT, 2, 0:8], 0.25 / (D_INNER // GROUPS), S["g_diag"])
                    z_gate()
                    silu(0)
                else:
                    dve.wait_ge(S["g_stat"], g + 1)
                    inverse_rms(Pb[0:TOKT, 2, 0:8], 0.25 / (D_INNER // GROUPS), S["g_diag"])
                pl = c_lin(i, "bc")
                done(pl)
                for t in range(2):
                    dve.scalar_tensor_tensor(cols(yT[:, t, :]), cols(yT[:, t, :]), small_of("gssm", g * 2 + t),
                                             lin_cols(pl), ALU.mult, ALU.mult).then_inc(S["g_val"], 1)
                for t in range(2):
                    dve.wait_ge(S["g_hi"], g * 2 + (t + 1))
                    dve.tensor_tensor(mid_lo[:, 5 + t, :], yT[:, t, :], mid_hi[:, 5 + t, :].bitcast(F32), ALU.subtract
                                      ).then_inc(S["g_ready"], 1)
                dve.nop().then_inc(S["lin_free"], 1)
                dve.wait_ge(S["state_out"], g * 16 + 16)
                if has_in:
                    silu(1)
                for m in range(8):
                    pl = c_lin(i, f"s{m}")
                    done(pl)
                    dve.tensor_tensor(cols(acc[:, m, :]), cols(acc[:, m, :]), lin_cols(pl), ALU.add
                                      ).then_inc(S["lin_free"], 1)
                    if has_in and m < 4:
                        conv(2 + m // 2, m % 2)
                    if has_in and m in (4, 6):
                        silu(m // 2)

            group(0)
            with dve.Fori(1, GROUPS) as i:
                chain.enter(i - 1, GROUP_LINKS)
                group(i)
            chain.leave(GROUPS - 1)
            group(GROUPS)
            dve.drain().then_inc(S["groups_over"], 1)

            for k in range(KT):
                dve.wait_ge(S["oa_hi"], k + 1)
                dve.tensor_tensor(mid_lo[:, k, 0:SEQ], o_attn[:, k, :], mid_hi[:, k, 0:SEQ].bitcast(F32), ALU.subtract
                                  ).then_inc(S["oa_ready"], 1)
            dve.wait_ge(S["groups_over"], 3)
            per = len(ROW_LIN)

            def row(i, odd):
                b = i * 2 + odd
                lo = 64 + 32 * odd
                one = bass.ds(b, 1)

                def pl_of(name):
                    return looped(LIN_D, 2 * per, i, odd * per + ROW_LIN.index(name))
                dve.tensor_copy(qlb[:, :, :], qlat[:, :, one, :].rearrange("p k o h -> p k (o h)"))
                dve.tensor_copy(qpb[lo:lo + 32, :], qpe_s[64:96, one, :].rearrange("p o h -> p (o h)"))
                dve.tensor_copy(snb[:, 0:2], ckv_s[:, :, one].rearrange("p k o -> p (k o)"))
                dve.tensor_copy(snb[lo:lo + 32, 2:3], kpe_s[64:96, one]).then_inc(S["qb_ready"], 1)
                dve.wait_ge(S["sc_done"], b + 1)
                link(dve.reduce_max(sms[0:16, 0:1], Pb[0:16, :, :].rearrange("p a b -> p (a b)"), AX.X))
                pl = pl_of("SN")
                done(pl)
                link(dve.tensor_tensor(sms[0:16, 1:2], lin[0:16, pl.slot, 0, 0:1], sms[0:16, 0:1], ALU.max))
                dve.tensor_copy(Pexp[0:16, PAST:PAST + 1], lin[0:16, pl.slot, 0, 0:1]).then_inc(S["lin_free"], 1)
                dve.tensor_scalar(sms[0:16, 2:3], sms[0:16, 1:2], -SM_SCALE, None, ALU.mult).then_inc(S["s_bias"], 1)
                dve.wait_ge(S["s_exp"], b + 1)
                link(dve.tensor_tensor(sms[0:16, 4:5], sms[0:16, 3:4], Pexp[0:16, PAST:PAST + 1], ALU.add))
                link(dve.reciprocal(sms[0:16, 5:6], sms[0:16, 4:5]))
                dve.tensor_scalar(pnd[:, :], ident[0:16, 0:16], Pexp[0:16, PAST:PAST + 1], sms[0:16, 5:6],
                                  ALU.mult, ALU.mult).then_inc(S["pn_ready"], 1)
                dve.wait_ge(S["ga_tanh"], b + 1)
                dve.nop().then_inc(S["lin_free"], 1)
                dve.wait_ge(S["gb_tanh"], b + 1)
                dve.scalar_tensor_tensor(at_g(acc, b), tg[:, :], 1.0, at_g(acc, b), ALU.add, ALU.mult
                                         ).then_inc(S["lin_free"], 1)
                pl = pl_of("PT")
                done(pl)
                dve.tensor_copy(PTs[:, :, :], lin[:, pl.slot, 0, 0:256].rearrange("p (j h) -> p j h", j=PAGES)
                                ).then_inc(S["lin_free"], 1)
                pl = pl_of("OL")
                done(pl)
                dve.wait_ge(S["lin_free"], pl_of("gb").index + 1)
                dve.tensor_scalar(ol_sb, lin[0:16, pl.slot, 0, 0:256], sms[0:16, 5:6], None, ALU.mult
                                  ).then_inc(S["lin_free"], 1)
                pl = pl_of("OT")
                done(pl)
                link(dve.tensor_copy(pnb[:, :], lin[:, pl.slot, 1, 0:16]))
                for k in range(2):
                    ol = dve.scalar_tensor_tensor(olat[:, k, one, :].rearrange("p o h -> p (o h)"), pnb[:, :],
                                                  ckv_s[:, k, one], lin[:, pl.slot, 0, 16 * k:16 * k + 16],
                                                  ALU.mult, ALU.add)
                ol.then_inc(S["lin_free"], 1)

            with dve.Fori(0, NB // 2) as i:
                chain.enter(i, ROW_LINKS)
                for odd in range(2):
                    row(i, odd)
            chain.leave(NB // 2)
            dve.wait_ge(S["olat_hi_s"], 1)
            dve.tensor_tensor(olat_lo[:, :], olat[:, :, :, :].rearrange("p k b h -> p (k b h)"),
                              olat_hi[:, :].bitcast(F32), ALU.subtract).then_inc(S["olat_ready"], 1)
            for h in range(2):
                dve.wait_ge(S["ov_hi"], h + 1)
                src = lin[64 * h:64 * h + 64, LIN_OV % 2, 0, 0:128].rearrange("p (k b h) -> p k b h", k=8, h=2)
                dve.tensor_tensor(mid_lo[64 * h:64 * h + 64, :, SEQ:T], src[:, :, :, h],
                                  mid_hi[64 * h:64 * h + 64, :, SEQ:T].bitcast(F32), ALU.subtract
                                  ).then_inc(S["ov_ready"], 1)
            dve.wait_ge(S["ov_ready"], 2)
            dve.nop().then_inc(S["lin_free"], 1)
            with dve.Fori(0, KT // 2) as i:
                for j in range(2):
                    pl = looped(LIN_E, 2, i, j)
                    m = i * 2 + j
                    done(pl)
                    dve.scalar_tensor_tensor(cols(etmp[:, j, :]), cols(at_g(sga, m)), 1.0, lin_cols(pl),
                                             ALU.add, ALU.mult).then_inc(S["lin_free"], 1)
                    dve.wait_ge(S["lin_free"], pl.index + 1)
                    dve.tensor_tensor(etmp[:, j, :], etmp[:, j, :], at_g(acc, m), ALU.add).then_inc(S["mg_val"], 1)
                    dve.wait_ge(S["mg_hi"], i * 2 + (j + 1))
                    dve.tensor_tensor(at_g(act_lo, m), etmp[:, j, :], at_g(act_hi, m).bitcast(F32), ALU.subtract
                                      ).then_inc(S["mg_ready"], 1)
            dve.memset(acc[:, :, :], 0.0)
            link(dve.memset(sqsum[:, 0, :], 0.0))
            with dve.Fori(0, KT // 2) as i:
                for j in range(2):
                    pl = looped(LIN_F, 2, i, j)
                    dve.wait_ge(S["mix_sq"], i * 2 + (j + 1))
                    dve.tensor_copy(cols(at_g(mix, i * 2 + j)), lin_cols(pl)).then_inc(S["lin_free"], 1)
                    dve.tensor_tensor(sqsum[:, 0, :], sqsum[:, 0, :], at_g(sq2, i * 2 + j), ALU.add
                                      ).then_inc(S["mix_sum"], 1)
                    dve.wait_ge(S["mix_sum"], i * 2 + (j + 1))
            dve.wait_ge(S["n_stat"], 1)
            inverse_rms(Pb[0:TOKT, 0, 0:8], 0.25 / D_MODEL, S["n_diag"])
            dve.wait_ge(S["x_again"], 16 * 4)
            pl = fixed(LIN_N)
            done(pl)
            for k in range(KT):
                link(dve.scalar_tensor_tensor(cols(mix[:, k, :]), cols(mix[:, k, :]), small_of("gpost", k),
                                              lin_cols(pl), ALU.mult, ALU.mult))
                dve.tensor_tensor(x2[:, k, :], x2[:, k, :], mix[:, k, :], ALU.add).then_inc(S["x2_val"], 1)
            dve.nop().then_inc(S["lin_free"], 1)
            dve.wait_ge(S["n_stat"], 2)
            inverse_rms(Pb[0:TOKT, 0, 8:16], 1.0 / D_MODEL, S["n_diag"])
            normed(KT, lambda k: x2[:, k, :], lambda k: small_of("gpremlp", k), fixed(LIN_N + 1), lambda k: mix[:, k, :],
                   lambda k: act_hi[:, k, :], lambda k: act_lo[:, k, :], S["h_val"], S["h_hi"], S["h_ready"], 0)

            def up(lin_at, blk_slot, blk):
                for j in range(4):
                    pl = lin_at(j)
                    dve.wait_ge(S["relu_a"], blk * 4 + (j + 1))
                    dve.tensor_tensor(cols(relu[:, j % 2, :]), lin_cols(pl), cols(relu[:, j % 2, :]), ALU.mult
                                      ).then_inc(S["lin_free"], 1)
                    dve.wait_ge(S["f_hi"], blk * 4 + (j + 1))
                    dve.tensor_tensor(mid_lo[:, 4 * blk_slot + j, :], relu[:, j % 2, :],
                                      mid_hi[:, 4 * blk_slot + j, :].bitcast(F32), ALU.subtract
                                      ).then_inc(S["f_ready"], 1)

            def square_sum(k):
                dve.wait_ge(S["acc_sq"], k + 1)
                if k == 0:
                    dve.tensor_copy(sqsum[:, 0, :], sq2[:, 0, :]).then_inc(S["acc_sum"], 1)
                else:
                    dve.tensor_tensor(sqsum[:, 0, :], sqsum[:, 0, :], sq2[:, k, :], ALU.add
                                      ).then_inc(S["acc_sum"], 1)
                dve.wait_ge(S["acc_sum"], k + 1)

            def down(lin_at, last=False):
                for m in range(8):
                    pl = lin_at(m)
                    done(pl)
                    dve.tensor_tensor(cols(acc[:, m, :]), cols(acc[:, m, :]), lin_cols(pl), ALU.add
                                      ).then_inc(S["lin_free"], 1)
                    if last and m:
                        square_sum(m - 1)
                if last:
                    square_sum(7)

            up(lambda j: fixed(LIN_G + j), 0, 0)
            with dve.Fori(0, 3) as i:
                for j in range(2):
                    la = LIN_G + 4 + 12 * j
                    up(lambda k: looped(la, 24, i, k), 1 - j, i * 2 + (j + 1))
                    down(lambda k: looped(la + 4, 24, i, k))
            la = LIN_G + 76
            up(lambda k: fixed(la + k), 1, 7)
            down(lambda k: fixed(la + 4 + k))
            down(lambda k: fixed(la + 12 + k), last=True)
            dve.wait_ge(S["n_stat"], 3)
            inverse_rms(Pb[0:TOKT, 0, 0:8], 1.0 / D_MODEL, S["n_diag"])
            pl = fixed(LIN_H)
            done(pl)
            for k in range(KT):
                link(dve.scalar_tensor_tensor(cols(mix[:, k, :]), cols(acc[:, k, :]), small_of("gpostmlp", k),
                                              lin_cols(pl), ALU.mult, ALU.mult))
                dve.tensor_tensor(mix[:, k, :], mix[:, k, :], x2[:, k, :], ALU.add).then_inc(S["y_val"], 1)


INS = ["wall", "xT", "small", "ident", "amask", "smask", "ropet", "pages", "cache", "rope", "hist", "state"]
OUTS = {"yT": [P, KT, T], "kvT": [P, 2, T], "kpeT": [ROPE, T], "convT": [GROUPS, P, 4, RAWW - SEQ],
        "ssmT": [GROUPS, P, 256], "stateT": [NB, SSM_HEADS, 64, STATE]}


def tiles(w):
    return w.reshape(-1, P, w.shape[1]).transpose(1, 0, 2)


def weight_stream(w_in, w_uq, w_uk, w_uv, w_br_attn, w_br_ssm, w_out, w_up, w_down):
    b = np.cumsum([0, Q_LORA, KV_LORA, ROPE, D_INNER, CONV_DIM, SSM_HEADS, D_MODEL, D_MODEL])
    w = {n: w_in[:, b[k]:b[k + 1]] for k, n in enumerate(["q", "kv", "pe", "z", "xbc", "dt", "ga", "gb"])}
    wall = np.zeros((N_CHUNKS, P, 1024), np.float32)
    n = [0]

    def put(*parts):
        at = 0
        for x in parts:
            x = x.reshape(P, -1)
            wall[n[0], :, at:at + x.shape[1]] = x
            at += x.shape[1]
        n[0] += 1

    def cols_of(x, a):
        return tiles(x[:, a:a + P])

    pe = w["pe"]
    put(tiles(np.concatenate([w["dt"], np.zeros((D_MODEL, 32), np.float32), pe, pe[:, 16:32], pe[:, 0:16]], axis=1)))
    for k in range(3):
        put(cols_of(w["q"], k * P))
    for k in range(2):
        put(cols_of(w["kv"], k * P))

    def group_in(name, g):
        if name[0] == "x":
            put(cols_of(w["xbc"], 256 * g + P * int(name[1])))
        elif name in "bc":
            put(cols_of(w["xbc"], D_INNER + 1024 * "bc".index(name) + P * g))
        else:
            put(cols_of(w["z"], 256 * g + P * int(name[1])))

    def group_rest(name, g):
        if name == "UQ":
            u = w_uq[:, 2 * g:2 * g + 2, :]
            u = np.concatenate([u, u[:, :, 80:96], u[:, :, 64:80]], axis=2)
            put(tiles(u.reshape(Q_LORA, 256)))
        elif name == "UKV":
            uk = w_uk[:, 2 * g:2 * g + 2, :].reshape(KV_LORA, P)
            uv = w_uv[:, 2 * g:2 * g + 2, :].reshape(KV_LORA, P)
            put(tiles(uk), uk.T, tiles(uv))
        else:
            m0 = 512 * "AB".index(name[1])
            put(tiles(w_br_ssm[256 * g:256 * g + 256, m0:m0 + 512]))

    for i in range(GROUPS + 1):
        order = FIRST_CH if i == 0 else (LAST_CH if i == GROUPS else STEADY_CH)
        for name in order:
            if name in IN_LIN:
                group_in(name, i)
            else:
                group_rest(name, i - 1)
    for m in range(KT):
        put(cols_of(w["ga"], m * P))
        put(cols_of(w["gb"], m * P))
    for half in range(2):
        put(*[tiles(w_uv[:, 2 * pr:2 * pr + 2, :].reshape(KV_LORA, P)) for pr in range(4 * half, 4 * half + 4)])
    for wt in (w_br_attn, w_out):
        for m in range(KT):
            put(cols_of(wt, m * P))

    def up(blk):
        for j in range(4):
            put(cols_of(w_up, (4 * blk + j) * P))

    def down(blk):
        for m in range(4):
            put(tiles(w_down[512 * blk:512 * blk + 512, 256 * m:256 * m + 256]))

    up(0)
    for blk in range(7):
        up(blk + 1)
        down(blk)
    down(7)
    assert n[0] == N_CHUNKS, n
    return wall


def lay_out(x):
    a = {k: np.asarray(v) for k, v in x.items()}
    w = {k: a[k][0] for k in ("w_in", "w_uq", "w_uk", "w_uv", "w_br_attn", "w_br_ssm", "w_out", "w_up", "w_down")}
    out = {"wall": weight_stream(**w)}
    tok = np.concatenate([a["x_prompt"][0], a["x_sample"][:, 0]], axis=0)
    out["xT"] = tiles(tok.T)
    ch = {"x0": 0, "x1": P}
    conv = np.concatenate([a["w_conv"][0], a["b_conv"][0][None]], axis=0).T
    chan = np.array([[[256 * g + c for c in range(P)], [256 * g + P + c for c in range(P)],
                      [D_INNER + P * g + c for c in range(P)],
                      [D_INNER + 1024 + P * g + c for c in range(P)]] for g in range(GROUPS)])
    vec = {"gpre": a["g_pre_mix"][0], "gq": a["g_q"][0], "gkv": a["g_kv"][0], "gssm": a["g_ssm"][0],
           "gpost": a["g_post_mix"][0], "gpremlp": a["g_pre_mlp"][0], "gpostmlp": a["g_post_mlp"][0],
           "dskip": np.repeat(a["d_skip"][0], 64)}
    small = np.zeros((P, N_SMALL), np.float32)
    for name, (at, n) in SMALL.items():
        if name in vec:
            small[:, at:at + n] = vec[name].reshape(n, P).T
    small[0:32, SMALL["dtbias"][0]] = a["dt_bias"][0]
    small[0:32, SMALL["alog"][0]] = a["a_log"][0]
    at, n = SMALL["conv"]
    small[:, at:at + n] = conv[chan].transpose(2, 0, 1, 3).reshape(P, n)
    out["small"] = small
    i = np.arange(P)
    out["ident"] = np.eye(P, dtype=np.float32)
    out["amask"] = np.where(i[None, :] <= i[:, None], 0, NEG).astype(np.float32)
    out["smask"] = np.where(i[:, None] <= i[None, :], 0, NEG).astype(np.float32)
    half = ROPE // 2
    inv = (np.float32(10000.0) ** (-np.arange(half, dtype=np.float32) / np.float32(half))).astype(np.float32)
    pos = np.concatenate([np.arange(SEQ), np.full(NB, PAST)]).astype(np.float32)
    ang = (inv[:, None] * pos[None, :]).astype(np.float32)
    rt = np.zeros((P, T), np.float32)
    rt[64:80] = rt[80:96] = np.cos(ang)
    rt[96:112] = -np.sin(ang)
    rt[112:128] = np.sin(ang)
    out["ropet"] = rt
    out["pages"] = a["page_table"].reshape(1, -1)
    c = a["cache_kv_latent"][0]
    out["cache"] = np.concatenate([c.transpose(0, 2, 1).reshape(N_PHYS, 2, P, PAGE).transpose(0, 2, 1, 3)
                                   .reshape(N_PHYS, P, 256), c], axis=2)
    out["rope"] = a["cache_k_rope"][0].transpose(0, 2, 1)
    past = a["state_conv"][0]
    hist = np.zeros((GROUPS, P, 4, NB, 4), np.float32)
    hist[..., 0:3] = past.transpose(2, 0, 1)[chan].transpose(0, 2, 1, 3, 4)
    out["hist"] = hist.reshape(GROUPS, P, 4, 4 * NB)
    out["state"] = a["state_ssm"][0]
    return {k: np.ascontiguousarray(v) for k, v in out.items()}, chan


def give_back(r, chan):
    y = r["yT"].transpose(2, 1, 0).reshape(T, D_MODEL)
    kv = r["kvT"].transpose(2, 1, 0).reshape(T, KV_LORA)
    pe = r["kpeT"].T
    conv = np.zeros((CONV_DIM, RAWW - SEQ), np.float32)
    conv[chan.reshape(-1)] = r["convT"].transpose(0, 2, 1, 3).reshape(-1, RAWW - SEQ)
    rows = conv[:, 3:].reshape(CONV_DIM, NB, 4)[:, :, 1:4]
    ssm = r["ssmT"].reshape(GROUPS, STATE, HPG, 64).transpose(0, 2, 3, 1).reshape(SSM_HEADS, 64, STATE)
    out = (y[:SEQ][None], y[SEQ:][:, None], kv[:SEQ][None, None], pe[:SEQ][None, None], ssm[None, None],
           conv[:, 0:3].T[None, None], kv[SEQ:][None, :, None], pe[SEQ:][None, :, None], r["stateT"][None],
           rows.transpose(1, 2, 0)[None])
    return tuple(np.ascontiguousarray(x) for x in out)


def build(nc, arrays):
    d = {n: nc.dram_tensor("in_" + n, arrays[n].shape, mybir.dt.from_np(arrays[n].dtype), kind="ExternalInput").ap()
         for n in INS}
    o = {n: nc.dram_tensor("out_" + n, tuple(shape), F32, kind="ExternalOutput").ap() for n, shape in OUTS.items()}
    build_layer(nc, d, o)


def kernel(**inputs):
    import concourse.bacc as bacc
    from concourse.bass_utils import run_bass_kernel_spmd
    arrays, chan = lay_out(inputs)
    nc = bacc.Bacc("TRN2", target_bir_lowering=False, num_devices=1)
    build(nc, arrays)
    r = run_bass_kernel_spmd(nc, [{"in_" + n: arrays[n] for n in INS}], core_ids=[0])
    return give_back({n: r.results[0]["out_" + n] for n in OUTS}, chan)
```
